# Optimizing a Trainium2 kernel written in Bass

```python
import jax, jax.numpy as jnp
from jax import lax
import numpy as np

D_MODEL = 1024
BATCH = 1
SEQ = 256
DEPTH = 1

D_MIX = D_MODEL
HEAD_DIM = 64
G_WIDTH = D_MIX // 4
R_WIDTH = 3 * D_MIX // 8
M_WIDTH = D_MIX - G_WIDTH - R_WIDTH
G_HEADS = G_WIDTH // HEAD_DIM
R_HEADS = R_WIDTH // HEAD_DIM
M_HEADS = M_WIDTH // HEAD_DIM
CHUNK = 128
W_LORA = 64
A_LORA = 64
G_LORA = 128
CONV_K = 3
G_PROJ = 2 * G_WIDTH
R_PROJ = 3 * R_WIDTH + W_LORA + A_LORA + G_LORA
M_PROJ = 4 * M_WIDTH + 4 * M_HEADS
P_IN = G_PROJ + R_PROJ + M_PROJ
N_EXPERTS = 32
TOP_K = 4
D_FF = D_MODEL
SWIGLU_LIMIT = 7.0
SWIGLU_ALPHA = 1.702
MOE_BLOCK = 256
LN_EPS = 1e-5
RWKV_GN_EPS = 64e-5
DEEPNORM_ALPHA = (2 * DEPTH) ** 0.25
DEEPNORM_BETA = (8 * DEPTH) ** -0.25

kernel_name = 'hybrid_gmlp_rwkv7_mlstm_moe_encoder'

def _head_norm(t, eps):
    t = t.astype(jnp.float32)
    mu = jnp.mean(t, -1, keepdims=True)
    var = jnp.mean(jnp.square(t - mu), -1, keepdims=True)
    return (t - mu) * lax.rsqrt(var + eps)

def _layer_norm(x, g, b):
    return (_head_norm(x, LN_EPS) * g + b).astype(x.dtype)

def _bidir(t):
    return jnp.stack([t, jnp.flip(t, axis=1)])

def _flip_bwd(t):
    return jnp.stack([t[0], jnp.flip(t[1], axis=1)])

def _merge_dirs(t):
    return t[0] + jnp.flip(t[1], axis=1)

def _centred_dwconv(x, w, b):
    r = w.shape[0] // 2
    sn = x.shape[1]
    xp = jnp.pad(x, ((0, 0), (r, r), (0, 0)))
    y = b
    for j in range(w.shape[0]):
        y = y + xp[:, j:j + sn] * w[j]
    return y

def gmlp_mixer(p, ln_g, ln_b, ws, bs):
    bn, sn, _ = p.shape
    p = jax.nn.gelu(p.astype(jnp.float32), approximate=False)
    u, v = p[..., :G_WIDTH], p[..., G_WIDTH:]
    v = _head_norm(v, LN_EPS) * ln_g + ln_b
    vc = v.reshape(bn, sn // CHUNK, CHUNK, G_HEADS, HEAD_DIM)
    y = jnp.einsum('hpq,bcqhe->bcphe', ws, vc) + jnp.transpose(bs)[None, None, :, :, None]
    return u * y.reshape(bn, sn, G_WIDTH)

def _wkv7_step(state, inp):
    r, w, k, v, a, b = inp
    sa = jnp.einsum('phvk,phk->phv', state, a)
    state = state * w[:, :, None, :] + sa[..., None] * b[:, :, None, :] + v[..., None] * k[:, :, None, :]
    return state, jnp.einsum('phvk,phk->phv', state, r)

def rwkv7_mixer(p, mu, w0, w2, a0, a2, g2, k_k, k_a, r_k, ln_g, ln_b):
    bn, sn, _ = p.shape
    pf = p.astype(jnp.float32)
    p_prev = jnp.pad(pf, ((0, 0), (1, 0), (0, 0)))[:, :-1]
    p_next = jnp.pad(pf, ((0, 0), (0, 1), (0, 0)))[:, 1:]
    pf = pf + mu[0] * (p_prev - pf) + mu[1] * (p_next - pf)
    o3 = 3 * R_WIDTH
    r, k, v, wd, ad, gd = jnp.split(pf, [R_WIDTH, 2 * R_WIDTH, o3, o3 + W_LORA, o3 + W_LORA + A_LORA], axis=-1)
    w_log = -jax.nn.softplus(-(w0[:, None, None] + jnp.einsum('bsr,drc->dbsc', jnp.tanh(wd), w2))) - 0.5
    decay = jnp.exp(-jnp.exp(w_log))
    iclr = jax.nn.sigmoid(a0[:, None, None] + jnp.einsum('bsr,drc->dbsc', ad, a2))
    gate = jax.nn.sigmoid(gd) @ g2
    hs = lambda t: t.reshape(t.shape[:-1] + (R_HEADS, HEAD_DIM))
    kk = hs(k * k_k)
    kk = kk / jnp.maximum(jnp.sqrt(jnp.sum(kk * kk, -1, keepdims=True)), 1e-12)
    k_dir = hs(k * (1.0 + (iclr - 1.0) * k_a))
    r_h, v_h = hs(r), hs(v)
    kk2 = _bidir(kk)
    tm = lambda t: jnp.moveaxis(t, 2, 0).reshape(sn, 2 * bn, R_HEADS, HEAD_DIM)
    xs = (tm(_bidir(r_h)), tm(_flip_bwd(hs(decay))), tm(_flip_bwd(k_dir)), tm(_bidir(v_h)),
          tm(-kk2), tm(kk2 * _flip_bwd(hs(iclr))))
    state0 = jnp.zeros((2 * bn, R_HEADS, HEAD_DIM, HEAD_DIM), jnp.float32)
    _, out = lax.scan(_wkv7_step, state0, xs)
    out = _merge_dirs(jnp.moveaxis(out.reshape(sn, 2, bn, R_HEADS, HEAD_DIM), 0, 2))
    out = _head_norm(out, RWKV_GN_EPS).reshape(bn, sn, R_WIDTH) * ln_g + ln_b
    bonus = jnp.sum(jnp.sum(r_h * k_dir * r_k, -1, keepdims=True), 0) * v_h
    return (out + bonus.reshape(bn, sn, R_WIDTH)) * gate

def mlstm_mixer(p, conv_w, conv_b, gate_b, ln_g):
    bn, sn, _ = p.shape
    nc = sn // CHUNK
    pf = p.astype(jnp.float32)
    qk, v, o, gates = jnp.split(pf, [2 * M_WIDTH, 3 * M_WIDTH, 4 * M_WIDTH], axis=-1)
    qk = jax.nn.silu(_centred_dwconv(qk, conv_w, conv_b))
    hs = lambda t: t.reshape(t.shape[:-1] + (M_HEADS, HEAD_DIM))
    q = hs(qk[..., :M_WIDTH])
    k = hs(qk[..., M_WIDTH:]) * HEAD_DIM ** -0.5
    v = hs(v)
    gates = (gates + gate_b).reshape(bn, sn, 2, 2, M_HEADS)
    ig = _flip_bwd(jnp.moveaxis(gates[:, :, 0], 2, 0))
    lf = _flip_bwd(jnp.moveaxis(jax.nn.log_sigmoid(gates[:, :, 1]), 2, 0))
    ch = lambda t: t.reshape(2 * bn, nc, CHUNK, M_HEADS, HEAD_DIM).transpose(1, 0, 3, 2, 4)
    chg = lambda t: t.reshape(2 * bn, nc, CHUNK, M_HEADS).transpose(1, 0, 3, 2)
    xs = (ch(_bidir(q)), ch(_bidir(k)), ch(_bidir(v)), chg(ig), chg(lf))
    tril = jnp.tril(jnp.ones((CHUNK, CHUNK), dtype=bool))

    def chunk_step(carry, inp):
        c_st, n_st, m_st = carry
        qc, kc, vc, igc, lfc = inp
        bcum = jnp.cumsum(lfc, axis=-1)
        dmat = jnp.where(tril, bcum[..., :, None] - bcum[..., None, :] + igc[..., None, :], -jnp.inf)
        inter = bcum + m_st[..., None]
        m_t = jnp.maximum(jnp.max(dmat, -1), inter)
        sc = jnp.einsum('phtd,phsd->phts', qc, kc) * jnp.exp(dmat - m_t[..., None])
        w_inter = jnp.exp(inter - m_t)
        num = jnp.einsum('phts,phsd->phtd', sc, vc) + w_inter[..., None] * jnp.einsum('phtd,phde->phte', qc, c_st)
        den = jnp.sum(sc, -1) + w_inter * jnp.einsum('phtd,phd->pht', qc, n_st)
        h = num / jnp.maximum(jnp.abs(den), jnp.exp(-m_t))[..., None]
        b_last = bcum[..., -1]
        lw = b_last[..., None] - bcum + igc
        m_new = jnp.maximum(b_last + m_st, jnp.max(lw, -1))
        wts = jnp.exp(lw - m_new[..., None])
        dec = jnp.exp(b_last + m_st - m_new)
        c_st = dec[..., None, None] * c_st + jnp.einsum('phs,phsd,phse->phde', wts, kc, vc)
        n_st = dec[..., None] * n_st + jnp.einsum('phs,phsd->phd', wts, kc)
        return (c_st, n_st, m_new), h

    carry0 = (jnp.zeros((2 * bn, M_HEADS, HEAD_DIM, HEAD_DIM), jnp.float32),
              jnp.zeros((2 * bn, M_HEADS, HEAD_DIM), jnp.float32),
              jnp.zeros((2 * bn, M_HEADS), jnp.float32))
    _, hseq = lax.scan(chunk_step, carry0, xs)
    hseq = hseq.transpose(1, 0, 3, 2, 4).reshape(2, bn, sn, M_HEADS, HEAD_DIM)
    h = _head_norm(_merge_dirs(hseq), LN_EPS).reshape(bn, sn, M_WIDTH) * ln_g
    return jax.nn.sigmoid(o) * h

def _moe(x, router_w, router_b, w1, b1, w2, b2):
    bn, sn, d = x.shape
    t = bn * sn
    xf = x.reshape(t, d)
    logits = (xf @ router_w).astype(jnp.float32) + router_b
    top_v, top_i = lax.top_k(logits, TOP_K)
    gate = jax.nn.softmax(top_v, axis=-1)
    na = t * TOP_K
    flat_e = top_i.reshape(na)
    flat_t = jnp.arange(na, dtype=jnp.int32) // TOP_K
    flat_g = gate.reshape(na)
    order = jnp.argsort(flat_e)
    se, st, sg = flat_e[order], flat_t[order], flat_g[order]
    counts = jnp.bincount(flat_e, length=N_EXPERTS)
    start = jnp.cumsum(counts) - counts
    pcounts = (counts + MOE_BLOCK - 1) // MOE_BLOCK * MOE_BLOCK
    pend = jnp.cumsum(pcounts)
    pstart = pend - pcounts
    dest = pstart[se] + jnp.arange(na, dtype=jnp.int32) - start[se]
    nb = -(-na // MOE_BLOCK) + N_EXPERTS
    row_t = jnp.zeros((nb * MOE_BLOCK,), jnp.int32).at[dest].set(st)
    row_g = jnp.zeros((nb * MOE_BLOCK,), jnp.float32).at[dest].set(sg)
    block_e = jnp.minimum(jnp.searchsorted(pend, jnp.arange(nb, dtype=jnp.int32) * MOE_BLOCK, side='right'), N_EXPERTS - 1)
    xs = xf[row_t].reshape(nb, MOE_BLOCK, d)

    def expert_block(args):
        xb, e = args
        hdn = xb @ w1[e] + b1[e]
        g_, u_ = hdn[:, :D_FF], hdn[:, D_FF:]
        g_ = jnp.minimum(g_, SWIGLU_LIMIT)
        u_ = jnp.clip(u_, -SWIGLU_LIMIT, SWIGLU_LIMIT)
        return ((u_ + 1.0) * (g_ * jax.nn.sigmoid(g_ * SWIGLU_ALPHA))) @ w2[e] + b2[e]

    ys = lax.map(expert_block, (xs, block_e)).reshape(nb * MOE_BLOCK, d)
    y = jnp.zeros((t, d), x.dtype).at[row_t].add((ys * row_g[:, None]).astype(x.dtype))
    return y.reshape(bn, sn, d)

def setup_inputs(seed: int = 0) -> dict:
    key = jax.random.key(seed)
    ks = iter(jax.random.split(key, 48))
    L = DEPTH
    nrm = lambda shape, s: jax.random.normal(next(ks), shape, jnp.float32) * s
    gain = lambda shape: 1.0 + nrm(shape, 0.1)
    x = nrm((BATCH, SEQ, D_MODEL), 1.0)
    w_in = nrm((L, D_MODEL, P_IN), D_MODEL ** -0.5)
    gmlp_ln_g = gain((L, G_WIDTH))
    gmlp_ln_b = nrm((L, G_WIDTH), 0.02)
    gmlp_ws = nrm((L, G_HEADS, CHUNK, CHUNK), CHUNK ** -0.5)
    gmlp_bs = gain((L, G_HEADS, CHUNK))
    rwkv_mu = jax.random.uniform(next(ks), (L, 2, R_PROJ), jnp.float32, 0.0, 0.5)
    rwkv_w0 = jax.random.uniform(next(ks), (L, 2, R_WIDTH), jnp.float32, -6.0, 1.0)
    rwkv_w2 = nrm((L, 2, W_LORA, R_WIDTH), 0.5 * W_LORA ** -0.5)
    rwkv_a0 = nrm((L, 2, R_WIDTH), 0.1)
    rwkv_a2 = nrm((L, 2, A_LORA, R_WIDTH), A_LORA ** -0.5)
    rwkv_g2 = nrm((L, G_LORA, R_WIDTH), G_LORA ** -0.5)
    rwkv_k_k = 0.85 + nrm((L, R_WIDTH), 0.1)
    rwkv_k_a = gain((L, R_WIDTH))
    rwkv_r_k = nrm((L, R_HEADS, HEAD_DIM), 0.1)
    rwkv_ln_g = gain((L, R_WIDTH))
    rwkv_ln_b = nrm((L, R_WIDTH), 0.02)
    mlstm_conv_w = nrm((L, CONV_K, 2 * M_WIDTH), CONV_K ** -0.5)
    mlstm_conv_b = nrm((L, 2 * M_WIDTH), 0.02)
    ib = nrm((L, 2, M_HEADS), 0.1)
    fb = jnp.linspace(3.0, 6.0, M_HEADS, dtype=jnp.float32) + nrm((L, 2, M_HEADS), 0.1)
    mlstm_gate_b = jnp.stack([ib, fb], axis=1).reshape(L, 4 * M_HEADS)
    mlstm_ln_g = gain((L, M_WIDTH))
    w_out = nrm((L, D_MIX, D_MODEL), DEEPNORM_BETA * D_MIX ** -0.5)
    ln1_g = gain((L, D_MODEL))
    ln1_b = nrm((L, D_MODEL), 0.02)
    router_w = nrm((L, D_MODEL, N_EXPERTS), D_MODEL ** -0.5)
    router_b = nrm((L, N_EXPERTS), 0.01)
    exp_w1 = nrm((L, N_EXPERTS, D_MODEL, 2 * D_FF), D_MODEL ** -0.5)
    exp_b1 = nrm((L, N_EXPERTS, 2 * D_FF), 0.02)
    exp_w2 = nrm((L, N_EXPERTS, D_FF, D_MODEL), DEEPNORM_BETA * D_FF ** -0.5)
    exp_b2 = nrm((L, N_EXPERTS, D_MODEL), 0.02)
    ln2_g = gain((L, D_MODEL))
    ln2_b = nrm((L, D_MODEL), 0.02)
    return {'x': x, 'w_in': w_in, 'gmlp_ln_g': gmlp_ln_g, 'gmlp_ln_b': gmlp_ln_b, 'gmlp_ws': gmlp_ws,
            'gmlp_bs': gmlp_bs, 'rwkv_mu': rwkv_mu, 'rwkv_w0': rwkv_w0, 'rwkv_w2': rwkv_w2,
            'rwkv_a0': rwkv_a0, 'rwkv_a2': rwkv_a2, 'rwkv_g2': rwkv_g2, 'rwkv_k_k': rwkv_k_k,
            'rwkv_k_a': rwkv_k_a, 'rwkv_r_k': rwkv_r_k, 'rwkv_ln_g': rwkv_ln_g, 'rwkv_ln_b': rwkv_ln_b,
            'mlstm_conv_w': mlstm_conv_w, 'mlstm_conv_b': mlstm_conv_b, 'mlstm_gate_b': mlstm_gate_b,
            'mlstm_ln_g': mlstm_ln_g, 'w_out': w_out, 'ln1_g': ln1_g, 'ln1_b': ln1_b,
            'router_w': router_w, 'router_b': router_b, 'exp_w1': exp_w1, 'exp_b1': exp_b1,
            'exp_w2': exp_w2, 'exp_b2': exp_b2, 'ln2_g': ln2_g, 'ln2_b': ln2_b}

def reference(x, w_in, gmlp_ln_g, gmlp_ln_b, gmlp_ws, gmlp_bs, rwkv_mu, rwkv_w0, rwkv_w2, rwkv_a0,
              rwkv_a2, rwkv_g2, rwkv_k_k, rwkv_k_a, rwkv_r_k, rwkv_ln_g, rwkv_ln_b, mlstm_conv_w,
              mlstm_conv_b, mlstm_gate_b, mlstm_ln_g, w_out, ln1_g, ln1_b, router_w, router_b,
              exp_w1, exp_b1, exp_w2, exp_b2, ln2_g, ln2_b):
    for l in range(DEPTH):
        proj = jnp.einsum('bsd,dp->bsp', x, w_in[l])
        pg, pr, pm = jnp.split(proj, [G_PROJ, G_PROJ + R_PROJ], axis=-1)
        y_g = gmlp_mixer(pg, gmlp_ln_g[l], gmlp_ln_b[l], gmlp_ws[l], gmlp_bs[l])
        y_r = rwkv7_mixer(pr, rwkv_mu[l], rwkv_w0[l], rwkv_w2[l], rwkv_a0[l], rwkv_a2[l], rwkv_g2[l],
                          rwkv_k_k[l], rwkv_k_a[l], rwkv_r_k[l], rwkv_ln_g[l], rwkv_ln_b[l])
        y_m = mlstm_mixer(pm, mlstm_conv_w[l], mlstm_conv_b[l], mlstm_gate_b[l], mlstm_ln_g[l])
        groups = jnp.concatenate([y_g.astype(x.dtype), y_r.astype(x.dtype), y_m.astype(x.dtype)], axis=-1)
        mix = jnp.einsum('bsc,cd->bsd', groups, w_out[l])
        x = _layer_norm(DEEPNORM_ALPHA * x + mix, ln1_g[l], ln1_b[l])
        ffn = _moe(x, router_w[l], router_b[l], exp_w1[l], exp_b1[l], exp_w2[l], exp_b2[l])
        x = _layer_norm(DEEPNORM_ALPHA * x + ffn, ln2_g[l], ln2_b[l])
    return x


_drawn_inputs = setup_inputs


def setup_inputs(seed=0):
    import zlib

    import numpy as np

    out = dict(_drawn_inputs(seed))
    spreads = {}
    factors = {'gmlp_ln_b': 4.6,
     'rwkv_w2': 4.585,
     'rwkv_a0': 3.976,
     'rwkv_k_k': 2.81,
     'rwkv_ln_b': 5.304,
     'mlstm_conv_b': 4.736,
     'router_b': 4.191,
     'exp_b1': 8.0,
     'exp_b2': 6.41,
     'ln2_b': 2.757}
    for name, (base, spread) in spreads.items():
        noise = np.random.default_rng([zlib.crc32(name.encode()), seed]).standard_normal(out[name].shape)
        drawn = base * np.exp(spread * noise) if base else spread * noise
        out[name] = __import__('jax').numpy.asarray(drawn.astype(out[name].dtype))
    for name, factor in factors.items():
        out[name] = (out[name] * factor).astype(out[name].dtype)
    return out
```

```python
import numpy as np
import concourse.bass as bass
from concourse import mybir
from contextlib import ExitStack

P = 128
D = 1024
S = 256
KD = D // P
NCH = S // P
HD = 64
RH = 6
RW = RH * HD
NP = RH // 2
GW = 256
NE = 32
TOPK = 4
SLOTS = 64
MAXPASS = S // SLOTS
F = 1024
R0 = 512
M0 = R0 + 3 * RW + 256
PIN = M0 + 4 * RW + 24
LEVELS = (2, 4, 8, 16, 32, 64)
KAPPA = float(np.exp(-0.5))
ALPHA = 2.0 ** 0.25
LN_EPS = 1e-5
GN_EPS = 64e-5
BIG = 1e30

C_ID, C_BONE = 0, 128
C_MASK2 = 256
C_GM = C_MASK2 + 512
C_X2 = C_GM + 2 * len(LEVELS) * P
C_HSEL = C_X2 + 2 * P
C_SELM = C_HSEL + 2
C_ONES = C_SELM + RH * P
C_IOTA = C_ONES + P
NCONST = C_IOTA + P


def constants():
    c = np.zeros((P, NCONST), np.float32)
    i = np.arange(P)
    row, col = i[:, None], i[None, :]
    c[:, C_ID:C_ID + P] = row == col
    c[:, C_BONE:C_BONE + P] = row // HD == col // HD
    for d in range(2):
        before = (row < col) if d == 0 else (row > col)
        c[:, C_MASK2 + 256 * d:C_MASK2 + 256 * d + P] = before
        c[:, C_MASK2 + 256 * d + P:C_MASK2 + 256 * d + 256] = before | (row == col)
        late, early = (row, col) if d == 0 else (col, row)
        for n, m in enumerate(LEVELS):
            off = (late // (2 * m) == early // (2 * m)) & (late // m % 2 == 1) & (early // m % 2 == 0)
            o = C_GM + (d * len(LEVELS) + n) * P
            c[:, o:o + P] = off | (row == col)
        late, early = early, late
        off = (late // 2 == early // 2) & (late % 2 == 1) & (early % 2 == 0)
        c[:, C_X2 + d * P:C_X2 + (d + 1) * P] = off | (row == col)
    c[:, C_HSEL:C_HSEL + 2] = row // HD == np.arange(2)[None, :]
    for h in range(RH):
        c[h, C_SELM + h * P:C_SELM + (h + 1) * P] = 1.0
    c[:, C_ONES:C_ONES + P] = 1.0
    c[:, C_IOTA:C_IOTA + P] = np.arange(P)[None, :] % SLOTS
    return c


ROWS = {}
_n = 0
for _name, _k in (("mu0", 11), ("mu1", 11), ("w0", 6), ("a0", 6), ("kk", 3), ("ka", 3), ("rk", 3),
                  ("cw", 18), ("cb", 6), ("bs", 4)):
    ROWS[_name] = _n
    _n += _k
NROWS = _n

T_TILES = ([("C", 0, "v", 2), ("C", 128, "wa", 0), ("C", 256, "gd", 0)]
           + [("A", 128 * i, "rk"[i // 3], i % 3) for i in range(4)]
           + [("B", 0, "k", 1), ("B", 128, "k", 2), ("B", 256, "v", 0), ("B", 384, "v", 1)]
           + [("D", 128 * i, "m", i) for i in range(4)] + [("E", 0, "m", 4), ("E", 128, "m", 5)])
MU_COL = {"r": 0, "k": 3, "v": 6, "wa": 9, "gd": 10}
NR = 11
NT = len(T_TILES)
PIECES = {"C": (R0 + 1024, 384, 2), "A": (R0, 512, 3), "B": (R0 + 512, 512, 4), "D": (M0, 512, 5),
          "E": (M0 + 512, 256, 0), "F": (M0 + 768, 384, 1), "G": (M0 + 1152, 408, 0), "H": (0, 512, 1)}
TOK_TILES = [(p, c) for p in "FGH" for c in range(NCH)]


def encoder_kernel(nc, t, out, dbg=None):
    f32 = mybir.dt.float32
    i32 = mybir.dt.int32
    ALU = mybir.AluOpType
    ACT = mybir.ActivationFunctionType
    X = mybir.AxisListType.X
    ctx = ExitStack()
    with ctx:
        def sem(name):
            return ctx.enter_context(nc.semaphore(name))

        SLOT = 4096
        ring = ctx.enter_context(nc.sbuf_tensor("ring", [P, 6 * SLOT], f32))
        POOLN = 28500
        pool_t = ctx.enter_context(nc.sbuf_tensor("pool", [P, POOLN], f32))
        bank = [ctx.enter_context(nc.psum_tensor(f"bank{i}", [P, 512], f32)) for i in range(8)]
        npass_i = ctx.enter_context(nc.sbuf_tensor("npass_i", [P, 1], i32))

        top = [0]

        def carve(n):
            o = top[0]
            top[0] += n
            assert top[0] <= POOLN, top[0]
            return o

        def view(o, *shape):
            n = int(np.prod(shape))
            a = pool_t[:, o:o + n]
            names = "abcd"[:len(shape)]
            if len(shape) == 1:
                return a
            return a.rearrange(f"p ({' '.join(names)}) -> p {' '.join(names)}",
                               **{k: v for k, v in zip(names[1:], shape[1:])})

        def rview(slot, o, *shape):
            n = int(np.prod(shape))
            a = ring[:, slot * SLOT + o:slot * SLOT + o + n]
            names = "abcd"[:len(shape)]
            if len(shape) == 1:
                return a
            return a.rearrange(f"p ({' '.join(names)}) -> p {' '.join(names)}",
                               **{k: v for k, v in zip(names[1:], shape[1:])})

        def pview(b, o, *shape):
            n = int(np.prod(shape))
            a = bank[b][:, o:o + n]
            names = "abcd"[:len(shape)]
            if len(shape) == 1:
                return a
            return a.rearrange(f"p ({' '.join(names)}) -> p {' '.join(names)}",
                               **{k: v for k, v in zip(names[1:], shape[1:])})

        def spread(a, n):
            return a.unsqueeze(len(a.shape)).broadcast_to(list(a.shape) + [n])

        cst = view(carve(NCONST), NCONST)
        x_tok = view(carve(2048), NCH, D)
        o_xT = carve(2048)
        xT = view(o_xT, KD, S)
        o_grp = carve(2048)
        grp = view(o_grp, NCH, D)
        pcol = view(carve(NROWS), NROWS)
        o_s = carve(1536)
        sigw = view(o_s, NP, 2, S)
        icl = view(carve(1536), NP, 2, S)
        o_kk = carve(768)
        kk = view(o_kk, NP, S)
        bon = view(carve(768), NP, S)
        o_m = top[0]
        rT = view(carve(768), NP, S)
        kT = view(carve(768), NP, S)
        o_vT = carve(768)
        vT = view(o_vT, NP, S)
        wa = view(carve(S), S)
        gd = view(carve(S), S)
        base = view(carve(2 * S), 2, S)
        wbuf = view(carve(512), 2, 4, HD)
        ubuf = view(carve(512), 2, 4, HD)
        hst = view(carve(2 * HD), 2, HD)
        vtok = view(carve(NCH * RW), NCH, RW)
        gate_r = view(carve(NCH * RW), NCH, RW)
        qk = view(carve(6 * S), 6, S)
        mv = view(carve(NCH * RH * 65), NCH, RH, 65)
        gel = view(carve(1024), NCH, 512)
        gt = view(carve(NCH * 24), NCH, 24)
        lnb = view(carve(2 * GW + 3 * RW), 2 * GW + 3 * RW)
        o_lora = carve(2 * RW)
        lora2 = view(o_lora, 2, RW)
        osig = view(o_lora, NCH, RW)
        g2 = view(carve(RW), RW)
        wsT = view(carve(512), 4, P)
        gbias = view(carve(4), 4)
        st1 = view(carve(16), 16)
        st2 = view(carve(16), 16)
        gcolm = view(carve(2 * NCH * RH), 2, NCH, RH)
        emt = view(carve(NCH * RH * 2), 2, NCH, RH)
        gam = view(carve(4), 2, 2)
        own = view(carve(11), 11)
        sref = view(carve(4), 2, NCH)
        den = view(carve(4), 2, NCH)
        rec = view(carve(4), 2, NCH)
        bsum = view(carve(NCH * RH), NCH, RH)
        mix_top = top[0]
        sgq = view(o_grp, 6, S)
        kkraw = rview(4, 0, NP, S)
        kksq = rview(4, 768, NP, S)
        orw = view(o_vT, NCH, RH, HD)
        hm = view(o_kk, NCH, RH, HD)
        ebuf_ = [view(o_s + 768 * b, 2, 384) for b in range(2)]
        pbuf = view(o_s + 1536, 2, 384)
        ntmp = view(o_s + 2304, 2, NCH, HD)
        row0 = view(o_xT, 2, S)
        row1 = view(o_xT + 512, 2, S)
        row2 = view(o_xT + 1024, 2, S)
        row3 = view(o_xT + 1536, 2, S)
        prow = view(o_xT, P)
        wsraw = view(o_xT + 128, 4, P)
        nqT = rview(2, 0, 2, 4, 256)
        mpT = rview(2, 2048, 2, 4, 256)
        xm = rview(3, 0, 2, 4, P)
        xmT = rview(3, 1024, 2, 4, P)
        gm = rview(3, 2048, 2, 4, P)
        bktok = rview(3, 3072, 2, 2, P)
        srel = rview(4, 0, 2, S)
        s_exc = rview(4, 512, 2, S)
        e_inc = rview(4, 1024, 2, S)
        e_inv = rview(4, 1536, 2, S)
        kdir = rview(4, 2048, 2, S)
        tmpk = rview(4, 2560, 2, S)
        rrk = rview(4, 3072, S)
        kka = rview(4, 3328, S)
        kds = rview(4, 3584, S)
        ar_ = [rview(5, 2048 * b, 2, NCH, 2, P) for b in range(2)]
        kt_ = [rview(5, 2048 * b + 1024, 2, NCH, P) for b in range(2)]
        bt_ = [rview(5, 2048 * b + 1536, 2, NCH, P) for b in range(2)]
        wout = [rview(h, 0, KD, 512) for h in range(2)]
        ln4 = view(o_s, 4, D)
        top[0] = o_m
        rw = view(carve(KD * NE), KD, NE)
        rb = view(carve(NE), NE)
        b2 = view(carve(D), D)
        lg = view(carve(NCH * NE), NCH, NE)
        mx = view(carve(NCH * 8), NCH, 8)
        mgt = view(carve(NCH * NE), NCH, NE)
        meq = view(carve(NCH * NE), NCH, NE)
        mcum = view(carve(NCH * NE), NCH, NE)
        msk = view(carve(NCH * NE), NCH, NE)
        gates = view(carve(NCH * NE), NCH, NE)
        gatesT = view(carve(S), S)
        posm = view(carve(NCH * (NE * MAXPASS + 1)), NCH, NE * MAXPASS + 1)
        gatex = view(carve(NCH * (NE * MAXPASS + 1)), NCH, NE * MAXPASS + 1)
        small = view(carve(32), 32)
        b1 = view(carve(2 * F), 2 * F)
        hot = view(carve(NE * MAXPASS + 1), NE * MAXPASS + 1)
        sel = view(carve(NCH * SLOTS), NCH, SLOTS)
        esel = view(carve(SLOTS), SLOTS)
        gsel = view(carve(NCH * P), NCH, P)
        xsr = view(carve(512), 512)
        xs = view(carve(512), 4, P)
        gT = view(carve(S), S)
        hr = view(carve(512), 512)
        ur = view(carve(512), 512)
        sg = view(carve(512), 512)
        hT = view(carve(512), 4, P)
        ysb = view(carve(512), 512)
        lnt = view(carve(2048), NCH, D)
        assert top[0] <= POOLN
        w1s = [rview(q, 0, 2, 2 * F) for q in range(4)]
        w2s = [rview(4 + h, 0, 4, D) for h in range(2)]

        ident = cst[:, C_ID:C_ID + P]
        bones = cst[:, C_BONE:C_BONE + P]
        ones = cst[:, C_ONES:C_ONES + P]
        hsel = cst[:, C_HSEL:C_HSEL + 2]

        def mask2(d):
            return cst[:, C_MASK2 + 256 * d:C_MASK2 + 256 * d + 256]

        def tri(d, inclusive):
            o = C_MASK2 + 256 * d + P * inclusive
            return cst[:, o:o + P]

        def gmask(d, n):
            o = C_GM + (d * len(LEVELS) + n) * P
            return cst[:, o:o + P]

        def par(name, i):
            return pcol[:, ROWS[name] + i:ROWS[name] + i + 1]

        LNO = {"gg": (0, GW), "gb": (GW, GW), "rg": (2 * GW, RW), "rb": (2 * GW + RW, RW),
               "mg": (2 * GW + 2 * RW, RW)}

        s_x = sem("x_loaded")
        s_par = sem("params_loaded")
        s_cst = sem("constants_loaded")
        s_small = sem("small_weights_loaded")
        s_lnb = sem("norm_rows_loaded")
        s_piece = {p: sem(f"w_in_{p}_loaded") for p in PIECES}
        s_wout = sem("w_out_loaded")
        s_late = sem("moe_small_loaded")
        s_ptr = sem("params_transposed")
        s_pev = sem("params_evacuated")
        s_xtr = sem("x_transposed")
        s_xev = sem("xT_evacuated")
        s_proj = sem("proj_tile_done")
        s_base = sem("proj_tile_read_by_act")
        s_shift = sem("proj_tile_shifted")
        s_lora = sem("lora_inputs_ready")
        s_z = sem("z_done")
        s_sig = sem("z_sigmoid_done")
        s_vtr = sem("v_transposed")
        s_vev = sem("vtok_evacuated")
        s_sq = sem("k_squares_ready")
        s_ss = sem("k_square_sums_done")
        s_kkd = sem("kk_ready")
        s_silu = sem("silu_sigmoid_done")
        s_rel = sem("decay_exponents_ready")
        s_exp = sem("decay_exps_done")
        s_ops = sem("scan_operands_ready")
        s_bon = sem("bonus_products_ready")
        s_prod = sem("products_done")
        s_prev = sem("products_evacuated")
        s_gps = sem("x2T_ready")
        s_x2 = sem("x2_transposed")
        s_xup = sem("x_evacuated")
        s_a = sem("level_product_done")
        s_g = sem("level_product_masked")
        s_xn = sem("level_update_done")
        s_bk = sem("bk_transposed")
        s_bkev = sem("bk_evacuated")
        s_w = sem("w_done")
        s_wev = sem("w_evacuated")
        s_u = sem("u_done")
        s_uev = sem("u_evacuated")
        s_h = sem("state_done")
        s_hev = sem("state_evacuated")
        s_o = sem("scan_out_done")
        s_oev = sem("scan_out_evacuated")
        s_gtr = sem("gate_rows_transposed")
        s_gact = sem("gate_exps_done")
        s_grow = sem("gate_rows_ready")
        s_gcol = sem("gate_cols_read")
        s_gcev = sem("stabilisers_ready")
        s_sc = sem("scores_done")
        s_mb = sem("m_rows_broadcast")
        s_arg = sem("decay_args_ready")
        s_de = sem("decay_factors_done")
        s_dm = sem("decay_factors_masked")
        s_pt = sem("weighted_scores_ready")
        s_pv = sem("num_den_done")
        s_hn = sem("mlstm_head_ready")
        s_gv = sem("gmlp_v_ready")
        s_gmix = sem("gmlp_mixed")
        s_bs = sem("gate_cols_and_bonus_sums_done")
        s_grp = sem("groups_ready")
        s_gT = sem("groups_transposed")
        s_gTe = sem("groupsT_evacuated")
        s_mix = sem("out_proj_done")
        s_x1 = sem("x1_ready")
        s_x1t = sem("x1_transposed")
        s_x1e = sem("x1T_evacuated")
        s_lg = sem("logits_done")
        s_rexp_in = sem("router_exp_ready")
        s_rexp = sem("router_exp_done")
        s_msk = sem("expert_mask_ready")
        s_pos = sem("positions_done")
        s_moe = sem("routing_ready")
        s_gtt = sem("gates_transposed")
        s_gte = sem("gatesT_evacuated")
        s_slot = [sem(f"slot{q}_loaded") for q in range(6)]
        s_sel = sem("selection_ready")
        s_gath = sem("tokens_gathered")
        s_xs = sem("tokens_evacuated")
        s_gts = sem("gate_selection_transposed")
        s_gtev = sem("gate_selection_evacuated")
        s_w1 = sem("w1_piece_used")
        s_hg = sem("gate_half_ready")
        s_hs = sem("gate_sigmoid_done")
        s_ht = sem("hidden_ready")
        s_w2 = sem("w2_piece_used")
        s_yev = sem("expert_out_evacuated")
        s_xsr = sem("token_rows_evacuated")
        s_all = sem("all_experts_combined")
        s_out = sem("out_stored")
        s_fin = sem("x2_ready")
        s_gsel = sem("gate_selection_ready")
        s_zero = sem("zeros_ready")
        s_one = sem("ones_ready")
        s_qk = sem("qk_ready")
        s_gtr2 = sem("tokens_transposed")
        s_htr = sem("hidden_transposed")
        s_htev = sem("hiddenT_evacuated")
        s_hu = sem("up_half_clipped")
        s_hm = sem("gate_half_done")
        s_x2r = sem("expert_residual_ready")
        s_var = sem("variances_ready")
        s_std = sem("deviations_ready")
        s_kmx = sem("k_square_sums_read")
        s_dch = sem("dve_step")
        s_ach = sem("act_step")
        s_pch = sem("pool_step")

        w_in = t["w_in"][0].rearrange("(k p) n -> p k n", p=P)
        w_out = t["w_out"][0].rearrange("(k p) n -> p k n", p=P)
        ew1 = t["exp_w1"][0].rearrange("e (k p) n -> e p k n", p=P)
        ew2 = t["exp_w2"][0].rearrange("e (k p) n -> e p k n", p=P)
        x_d = t["x"][0].rearrange("(c p) d -> p c d", p=P)
        out_d = out[0].rearrange("(c p) d -> p c d", p=P)

        def row_bc(a):
            return a.unsqueeze(0).broadcast_to([P, a.shape[0]])

        block = ctx.enter_context(nc.Block())

        @block.sync
        def _(sp):
            def load_piece(p):
                c0, n, slot = PIECES[p]
                sp.dma_start(rview(slot, 0, KD, n), w_in[:, :, c0:c0 + n]).then_inc(s_piece[p], 16)

            sp.dma_start(x_tok, x_d).then_inc(s_x, 16)
            for p in "CABDEF":
                load_piece(p)
            sp.wait_ge(s_proj, NT)
            load_piece("G")
            sp.wait_ge(s_proj, NT + 2)
            load_piece("H")
            sp.wait_ge(s_proj, NT + 4)
            sp.dma_start(wout[0], w_out[:, :, 0:512]).then_inc(s_wout, 16)
            sp.wait_ge(s_proj, NT + 6)
            sp.dma_start(wout[1], w_out[:, :, 512:1024]).then_inc(s_wout, 16)

            def load_slot(e, q):
                if q < 4:
                    dst, src = w1s[q], ew1[e][:, 2 * q:2 * q + 2]
                else:
                    dst, src = w2s[q - 4], ew2[e][:, 4 * (q - 4):4 * (q - 4) + 4]
                sp.dma_start(dst, src).then_inc(s_slot[q], 16)

            def reload(e, it):
                for q in range(4):
                    sp.wait_ge(s_w1, it * 4 + (q - 3))
                    load_slot(e, q)
                for q in range(4, 6):
                    sp.wait_ge(s_w2, it * 2 + (q - 5))
                    load_slot(e, q)

            sp.wait_ge(s_oev, 2 * NP)
            for q in (2, 3, 4, 5):
                load_slot(0, q)
            sp.wait_ge(s_mix, 4)
            for q in (0, 1):
                load_slot(0, q)
            with sp.Fori(1, NE) as e:
                reload(e, e)
            sp.wait_ge(s_moe, 2)
            npass = sp.value_load(npass_i[0:1, 0:1], min_val=1, max_val=MAXPASS)
            with sp.If(npass > 1):
                with sp.Fori(1, npass) as p:
                    with sp.Fori(0, NE) as e:
                        reload(e, p * NE + e)
            sp.wait_ge(s_fin, NCH)
            sp.dma_start(out_d, x_tok).then_inc(s_out, 16)
            sp.wait_ge(s_out, 16)
            if dbg is not None:
                sp.dma_start(dbg["grp"].rearrange("(c p) d -> p c d", p=P), grp).then_inc(s_out, 16)
                sp.wait_ge(s_out, 32)

        NPAR = 11

        @block.scalar
        def _(act):
            A = nc.scalar.activation
            roots = [0]
            act.dma_start(cst, t["consts"]).then_inc(s_cst, 16)
            rows = [("mu0", t["rwkv_mu"][0, 0:1]), ("mu1", t["rwkv_mu"][0, 1:2]), ("w0", t["rwkv_w0"][0]),
                    ("a0", t["rwkv_a0"][0]), ("kk", t["rwkv_k_k"]), ("ka", t["rwkv_k_a"]),
                    ("rk", t["rwkv_r_k"].rearrange("l h d -> l (h d)")), ("cw", t["mlstm_conv_w"][0]),
                    ("cb", t["mlstm_conv_b"]), ("bs", t["gmlp_bs"][0])]
            for name, src in rows:
                n = src.shape[0] * src.shape[1] // P
                act.dma_start(prow[ROWS[name]:ROWS[name] + n, :],
                              src.rearrange("a (n p) -> (a n) p", p=P)).then_inc(s_par, 16)
            act.dma_start(wsraw, t["gmlp_ws"][0].rearrange("h p q -> p h q")).then_inc(s_par, 16)
            act.dma_start(lora2[0:64], t["rwkv_w2"][0].rearrange("d r c -> r d c")).then_inc(s_small, 16)
            act.dma_start(lora2[64:128], t["rwkv_a2"][0].rearrange("d r c -> r d c")).then_inc(s_small, 16)
            act.dma_start(g2, t["rwkv_g2"][0]).then_inc(s_small, 16)
            act.dma_start(gbias[0:6, :], t["mlstm_gate_b"][0].rearrange("(k h) -> h k", h=RH),
                          allow_slow_non_contiguous=True).then_inc(s_small, 16)
            for k, src in (("gg", "gmlp_ln_g"), ("gb", "gmlp_ln_b"), ("rg", "rwkv_ln_g"), ("rb", "rwkv_ln_b"),
                           ("mg", "mlstm_ln_g")):
                o, n = LNO[k]
                act.dma_start(lnb[:, o:o + n], row_bc(t[src][0])).then_inc(s_lnb, 16)

            for g in range(4):
                act.wait_ge(s_xtr, g + 1)
                A(xT[:, 2 * g:2 * g + 2, :], pview(g, 0, 2, S), ACT.Copy).then_inc(s_xev, 1)

            def base_of(i):
                act.wait_ge(s_proj, i + 1)
                if i >= 2:
                    act.wait_ge(s_shift, i - 1)
                piece, col, kind, j = T_TILES[i]
                if i < NR:
                    if i == 0:
                        act.wait_ge(s_pev, 2)
                    m = MU_COL[kind] + (j if kind in "rkv" else 0)
                    A(base[:, i % 2], bank[i % 4][:, 0:S], ACT.Copy, scale=own[:, m:m + 1]).then_inc(s_base, 1)
                else:
                    A(base[:, i % 2], bank[i % 4][:, 0:S], ACT.Identity, bias=par("cb", j),
                      scale=par("cw", 6 + j)).then_inc(s_base, 1)

            def z_sigmoids(pt):
                act.wait_ge(s_z, pt + 1)
                b = 4 + 2 * (pt % 2)
                for d in range(2):
                    A(sigw[:, pt, d], bank[b][:, S * d:S * d + S], ACT.Sigmoid, bias=par("w0", 3 * d + pt))
                    last = A(icl[:, pt, d], bank[b + 1][:, S * d:S * d + S], ACT.Sigmoid,
                             bias=par("a0", 3 * d + pt))
                last.then_inc(s_sig, 1)

            for i in range(NR):
                base_of(i)
                if i == 3:
                    act.wait_ge(s_shift, 2)
                    A(wa[0:64], wa[0:64], ACT.Tanh).then_inc(s_lora, 1)
                if i == 4:
                    act.wait_ge(s_shift, 3)
                    A(gd, gd, ACT.Sigmoid).then_inc(s_lora, 1)
            z_sigmoids(0)
            z_sigmoids(1)
            base_of(11)
            base_of(12)
            z_sigmoids(2)
            base_of(13)
            base_of(14)
            act.wait_ge(s_kmx, 2)
            A(kk, kk, ACT.Sqrt).then_inc(s_kkd, 1)
            act.wait_ge(s_vtr, 1)
            A(vtok[:, 0], bank[4][:, 0:RW], ACT.Copy)
            A(vtok[:, 1], bank[5][:, 0:RW], ACT.Copy).then_inc(s_vev, 1)
            base_of(15)
            base_of(16)
            act.wait_ge(s_vtr, 2)
            A(gate_r[:, 0], bank[6][:, 0:RW], ACT.Copy)
            A(gate_r[:, 1], bank[7][:, 0:RW], ACT.Copy).then_inc(s_vev, 1)
            act.wait_ge(s_shift, NT)
            A(sgq, qk, ACT.Sigmoid).then_inc(s_silu, 1)
            for j in range(4):
                piece, c = TOK_TILES[j]
                act.wait_ge(s_proj, NT + j + 1)
                b = bank[(NT + j) % 4]
                if piece == "F":
                    A(mv[:, c, :, 0:HD], b[:, 0:RW].rearrange("p (h e) -> p h e", h=RH), ACT.Copy).then_inc(s_base, 1)
                else:
                    A(osig[:, c], b[:, 0:RW], ACT.Sigmoid)
                    A(gt[:, c], b[:, RW:RW + 24], ACT.Copy).then_inc(s_base, 1)

            def root(g):
                roots[0] += 1
                act.wait_ge(s_var, roots[0])
                A(st2[:, 0:g], st2[:, 0:g], ACT.Sqrt).then_inc(s_std, 1)

            def decay_exps(pt):
                act.wait_ge(s_rel, pt + 1)
                A(e_inv, srel, ACT.Exp, scale=KAPPA)
                A(e_inc, srel, ACT.Exp, scale=-KAPPA)
                A(gam[:, pt % 2], gam[:, pt % 2], ACT.Exp, scale=-KAPPA)
                A(s_exc, s_exc, ACT.Exp, scale=-KAPPA).then_inc(s_exp, 1)

            decay_exps(0)
            for j in (4, 5):
                act.wait_ge(s_proj, NT + j + 1)
                A(gel[:, j - 4], bank[(NT + j) % 4][:, 0:512], ACT.Gelu).then_inc(s_base, 1)
            act.wait_ge(s_grow, 1)
            A(row1[0:6], row1[0:6], ACT.Exp, scale=-1.0).then_inc(s_ach, 1)
            act.wait_ge(s_ach, 1)
            A(row1[0:6], row1[0:6], ACT.Ln, bias=1.0).then_inc(s_gact, 1)

            for pt in range(NP):
                for d in range(2):
                    act.wait_ge(s_bk, 2 * pt + d + 1)
                    A(bktok[:, d], pview(3 + 4 * d, 0, 2, P), ACT.Copy).then_inc(s_bkev, 1)
                    act.wait_ge(s_x2, 2 * pt + d + 1)
                    A(xm[:, d], pview(1 + 4 * d, 0, 4, P), ACT.Copy).then_inc(s_xup, 1)
                for n in range(len(LEVELS)):
                    for d in range(2):
                        act.wait_ge(s_xn, 12 * pt + 2 * n + d + 1)
                        if n < len(LEVELS) - 1:
                            A(xm[:, d], pview(1 + 4 * d, 0, 4, P), ACT.Copy)
                        A(xmT[:, d], pview(2 + 4 * d, 0, 4, P), ACT.Copy).then_inc(s_xup, 1)
                    if n == 3 and pt + 1 < NP:
                        decay_exps(pt + 1)
                    if n == 2 and pt + 1 == NP:
                        root(2)
                for step in range(2):
                    for d in range(2):
                        cu = d if step == 0 else 1 - d
                        act.wait_ge(s_u, 4 * pt + 2 * step + d + 1)
                        A(ubuf[:, d, cu::2], pview(3 + 4 * d, 256, 4, HD)[:, cu::2], ACT.Copy).then_inc(s_uev, 1)
                    if step == 0:
                        for d in range(2):
                            act.wait_ge(s_h, 2 * pt + d + 1)
                            A(hst[:, d], bank[4 * d][:, 0:HD], ACT.Copy,
                              scale=gam[:, pt % 2, d:d + 1]).then_inc(s_hev, 1)

            act.wait_ge(s_gcol, 1)
            A(emt, emt, ACT.Exp, scale=-1.0).then_inc(s_gcev, 1)
            for h in range(RH):
                act.wait_ge(s_arg, h + 1)
                A(ebuf_[h % 2], ebuf_[h % 2], ACT.Exp, scale=-1.0).then_inc(s_de, 1)

            root(NCH * RH)
            root(NCH * RH)
            for g in range(4):
                act.wait_ge(s_gT, g + 1)
                A(xT[:, 2 * g:2 * g + 2, :], pview(g, 0, 2, S), ACT.Copy).then_inc(s_gTe, 1)
            for c in range(NCH):
                root(1)
                for q in range(2):
                    act.wait_ge(s_x1t, 2 * c + q + 1)
                    A(xT[:, 4 * q:4 * q + 4, P * c:P * c + P], pview(2 * c + q, 0, 4, P), ACT.Copy).then_inc(s_x1e, 1)
            act.wait_ge(s_rexp_in, 1)
            for c in range(NCH):
                last = A(gates[:, c], lg[:, c], ACT.Exp, bias=small[:, c:c + 1])
            last.then_inc(s_rexp, 1)
            act.wait_ge(s_gtt, 1)
            A(gatesT[0:NE], bank[6][0:NE, 0:S], ACT.Copy).then_inc(s_gte, 1)

            act.wait_ge(s_gath, 1)
            A(xsr, bank[7][:, :], ACT.Copy).then_inc(s_xsr, 1)
            act.wait_ge(s_gtr2, 1)
            A(xs, pview(7, 0, 4, P), ACT.Copy).then_inc(s_xs, 1)
            act.wait_ge(s_moe, 2)
            npass = act.value_load(npass_i[0:1, 0:1], min_val=1, max_val=MAXPASS)
            with act.Fori(0, npass) as p:
                with act.Fori(0, NE) as e:
                    it = p * NE + e
                    act.wait_ge(s_gts, it + 1)
                    A(gT, bank[6][:, 0:S], ACT.Copy).then_inc(s_gtev, 1)
                    act.wait_ge(s_gath, it + 2)
                    A(xsr, bank[7][:, :], ACT.Copy).then_inc(s_xsr, 1)
                    act.wait_ge(s_hg, it + 1)
                    A(sg, hr, ACT.Sigmoid, scale=1.702).then_inc(s_hs, 1)
                    act.wait_ge(s_gtr2, it + 2)
                    A(xs, pview(7, 0, 4, P), ACT.Copy).then_inc(s_xs, 1)
                    act.wait_ge(s_htr, it + 1)
                    A(hT, pview(4, 0, 4, P), ACT.Copy).then_inc(s_htev, 1)
                    act.wait_ge(s_w2, it * 2 + 2)
                    A(ysb, bank[6][:, :], ACT.Copy).then_inc(s_yev, 1)
            root(1)
            root(1)

        @block.tensor
        def _(pe):
            mm = nc.tensor.matmul
            tr = nc.tensor.transpose
            pe.wait_ge(s_cst, 16)
            pe.wait_ge(s_par, 16 * NPAR)
            tr(bank[4][:, 0:NROWS], prow[0:NROWS, :], ident[0:NROWS, 0:NROWS])
            for g in range(4):
                last = tr(bank[5][:, P * g:P * g + P], wsraw[:, g], ident)
            last.then_inc(s_ptr, 1)
            pe.wait_ge(s_x, 16)
            for g in range(4):
                for k in range(2):
                    for c in range(NCH):
                        last = tr(pview(g, 0, 2, S)[:, k, P * c:P * c + P],
                                  x_tok[:, c, P * (2 * g + k):P * (2 * g + k + 1)], ident)
                last.then_inc(s_xtr, 1)
            pe.wait_ge(s_xev, 4)

            loaded = []

            def piece_ready(p):
                if p not in loaded:
                    pe.wait_ge(s_piece[p], 16)
                    loaded.append(p)

            def bank_free(i):
                if i >= 4:
                    if i - 4 < NT:
                        pe.wait_ge(s_shift, i - 3)
                    else:
                        pe.wait_ge(s_base, i - 3)

            def t_tile(i):
                p, col, _, _ = T_TILES[i]
                piece_ready(p)
                bank_free(i)
                w = rview(PIECES[p][2], 0, KD, PIECES[p][1])
                for k in range(KD):
                    last = mm(bank[i % 4][:, 0:S], w[:, k, col:col + P], xT[:, k], start=(k == 0), stop=(k == KD - 1))
                last.then_inc(s_proj, 1)

            def tok_tile(j):
                p, c = TOK_TILES[j]
                piece_ready(p)
                bank_free(NT + j)
                n = PIECES[p][1]
                w = rview(PIECES[p][2], 0, KD, n)
                for k in range(KD):
                    last = mm(bank[(NT + j) % 4][:, 0:n], xT[:, k, P * c:P * c + P], w[:, k, :],
                              start=(k == 0), stop=(k == KD - 1))
                last.then_inc(s_proj, 1)

            def z_tiles(pt):
                b = 4 + 2 * (pt % 2)
                if pt == 2:
                    pe.wait_ge(s_sig, 1)
                for d in range(2):
                    mm(bank[b][:, S * d:S * d + S], lora2[0:64, d, P * pt:P * pt + P], wa[0:64], start=True, stop=True)
                for d in range(2):
                    last = mm(bank[b + 1][:, S * d:S * d + S], lora2[64:128, d, P * pt:P * pt + P], wa[64:128],
                              start=True, stop=True)
                last.then_inc(s_z, 1)

            for i in range(NR):
                t_tile(i)
            pe.wait_ge(s_lora, 1)
            pe.wait_ge(s_small, 64)
            pe.wait_ge(s_pev, 1)
            z_tiles(0)
            z_tiles(1)
            t_tile(11)
            t_tile(12)
            z_tiles(2)
            pe.wait_ge(s_sig, 2)
            pe.wait_ge(s_sq, 1)
            kf = kksq.rearrange("p a s -> p (a s)")
            mm(bank[6][:, 0:512], bones, kf[:, 0:512], start=True, stop=True)
            mm(bank[7][:, 0:S], bones, kf[:, 512:768], start=True, stop=True).then_inc(s_ss, 1)
            t_tile(13)
            t_tile(14)
            pe.wait_ge(s_sig, 3)
            for c in range(NCH):
                for pt in range(NP):
                    last = tr(bank[4 + c][:, P * pt:P * pt + P], vT[:, pt, P * c:P * c + P], ident)
            last.then_inc(s_vtr, 1)
            t_tile(15)
            t_tile(16)
            pe.wait_ge(s_kmx, 2)
            pe.wait_ge(s_lora, 2)
            for c in range(NCH):
                last = mm(bank[6 + c][:, 0:RW], gd[:, P * c:P * c + P], g2, start=True, stop=True)
            last.then_inc(s_vtr, 1)
            for j in range(6):
                tok_tile(j)
            pe.wait_ge(s_base, NT + 4)
            pe.wait_ge(s_vev, 1)
            for k in range(4):
                for c in range(NCH):
                    last = tr(bank[4 + k // 2][0:RH, S * (k % 2) + P * c:S * (k % 2) + P * c + P],
                              gt[:, c, RH * k:RH * k + RH], ident)
            last.then_inc(s_gtr, 1)

            pe.wait_ge(s_base, NT + 6)
            pe.wait_ge(s_vev, 2)
            pe.wait_ge(s_grow, 1)
            for pt in range(NP):
                ar, kt, bt = ar_[pt % 2], kt_[pt % 2], bt_[pt % 2]
                pe.wait_ge(s_ops, pt + 1)
                if pt:
                    pe.wait_ge(s_oev, 2 * pt)
                for d in range(2):
                    for b, op in ((4 * d, kt), (4 * d + 2, bt)):
                        for j in range(4):
                            h, c = j // 2, j % 2
                            hp = slice(HD * h, HD * h + HD)
                            last = mm(bank[b + j // 2][:, 256 * (j % 2):256 * (j % 2) + 256], op[hp, d, c],
                                      ar[hp, d, c].rearrange("p a t -> p (a t)"), start=True, stop=True)
                        last.then_inc(s_prod, 1)
                for d in range(2):
                    pe.wait_ge(s_prev, 4 * pt + 2 * d + 2)
                    tr(pview(3 + 4 * d, 0, 2, P)[:, 0], bt[:, d, d], ident)
                    tr(pview(3 + 4 * d, 0, 2, P)[:, 1], kt[:, d, d], ident).then_inc(s_bk, 1)
                    pe.wait_ge(s_gps, 2 * pt + d + 1)
                    for j in range(4):
                        last = tr(pview(1 + 4 * d, 0, 4, P)[:, j], xmT[:, d, j], ident)
                    last.then_inc(s_x2, 1)
                for n in range(len(LEVELS)):
                    for d in range(2):
                        pe.wait_ge(s_xup, 14 * pt + 2 * n + d + 1)
                        for j in range(4):
                            last = mm(pview(4 * d, 0, 4, P)[:, j], mpT[:, d, j, 0:P], xm[:, d, j], start=True, stop=True)
                        last.then_inc(s_a, 1)
                    for d in range(2):
                        pe.wait_ge(s_g, 12 * pt + 2 * n + d + 1)
                        for j in range(4):
                            if n < len(LEVELS) - 1:
                                mm(pview(1 + 4 * d, 0, 4, P)[:, j], xmT[:, d, j], gm[:, d, j], start=True, stop=True)
                            last = mm(pview(2 + 4 * d, 0, 4, P)[:, j], gm[:, d, j], xmT[:, d, j], start=True, stop=True)
                        last.then_inc(s_xn, 1)

                def w_of(d, h):
                    return bank[4 * d + 3 * (1 - h)][:, 192:192 + HD]

                def v_of(c, h):
                    return vtok[:, c, HD * (2 * pt + h):HD * (2 * pt + h) + HD]

                for step in range(2):
                    for d in range(2):
                        c = d if step == 0 else 1 - d
                        if step == 0:
                            pe.wait_ge(s_bkev, 2 * pt + d + 1)
                        else:
                            pe.wait_ge(s_hev, 2 * pt + d + 1)
                        for h in range(2):
                            j = 2 * h + c
                            hp = slice(HD * h, HD * h + HD)
                            w = w_of(d, h)
                            last = mm(w, nqT[:, d, j, 0:P], v_of(c, h), start=True, stop=(step == 0))
                            if step == 1:
                                last = mm(w, ar[hp, d, c, 0], hst[hp, d], start=False, stop=True)
                        last.then_inc(s_w, 1)
                    for d in range(2):
                        c = d if step == 0 else 1 - d
                        pe.wait_ge(s_wev, 4 * pt + 2 * step + d + 1)
                        if step == 0:
                            pe.wait_ge(s_xup, 14 * pt + 12 + d + 1)
                        for h in range(2):
                            j = 2 * h + c
                            last = mm(pview(3 + 4 * d, 256, 4, HD)[:, j], xmT[:, d, j], wbuf[:, d, j], start=True, stop=True)
                        last.then_inc(s_u, 1)
                    if step == 0:
                        for d in range(2):
                            pe.wait_ge(s_uev, 4 * pt + d + 1)
                            for h in range(2):
                                hp = slice(HD * h, HD * h + HD)
                                mm(bank[4 * d][hp, 0:HD], bktok[:, d, 0, hp], ubuf[:, d, 2 * h + d], start=True, stop=False)
                                last = mm(bank[4 * d][hp, 0:HD], bktok[:, d, 1, hp], v_of(d, h), start=False, stop=True)
                            last.then_inc(s_h, 1)
                pe.wait_ge(s_uev, 4 * pt + 4)
                for c in range(NCH):
                    for h in range(2):
                        j = 2 * h + c
                        hp = slice(HD * h, HD * h + HD)
                        o = bank[1 + 4 * c + h][:, 0:HD]
                        for d in range(2):
                            mm(o, mpT[:, d, j, P:2 * P], ubuf[:, d, j], start=(d == 0), stop=False)
                            if c == 1 - d:
                                mm(o, ar[hp, d, c, 1], hst[hp, d], start=False, stop=False)
                            last = mm(o, nqT[:, d, j, P:2 * P], v_of(c, h), start=False, stop=(d == 1))
                    last.then_inc(s_o, 1)

            pe.wait_ge(s_gv, 1)
            pe.wait_ge(s_oev, 2 * NP)
            for g in range(4):
                last = mm(pview(6, P * g, NCH, HD), wsT[:, g], gel[:, :, GW + HD * g:GW + HD * g + HD], start=True, stop=True)
            last.then_inc(s_gmix, 1)
            pe.wait_ge(s_grow, 2)
            for kind, r in ((0, row3), (1, row0)):
                for d in range(2):
                    for c in range(NCH):
                        i = 12 * (2 * kind + d) // 1 + RH * c
                        tr(bank[7][:, i:i + RH], r[0:RH, d, P * c:P * c + P], ident[0:RH, 0:RH])
            pe.wait_ge(s_bon, NP)
            for c in range(NCH):
                for pt in range(NP):
                    last = mm(bank[7][:, 64 + RH * c + 2 * pt:66 + RH * c + 2 * pt], bon[:, pt, P * c:P * c + P], hsel,
                              start=True, stop=True)
            last.then_inc(s_bs, 1)
            pe.wait_ge(s_qk, 1)
            pe.wait_ge(s_one, 1)

            def weigh(h):
                pe.wait_ge(s_pt, h + 1)
                if h >= 2:
                    pe.wait_ge(s_hn, h - 1)
                nd = pview(4 + h % 2, 0, 2, NCH, 65)
                for d, c, parts in ((0, 0, ((0, 0),)), (0, 1, ((0, P), (1, S))),
                                    (1, 0, ((0, 0), (1, P))), (1, 1, ((1, S),))):
                    for n, (sc, col) in enumerate(parts):
                        last = mm(nd[:, d, c], pbuf[:, d, col:col + P], mv[:, sc, h], start=(n == 0),
                                  stop=(n == len(parts) - 1))
                last.then_inc(s_pv, 1)

            for h in range(RH):
                pt = h // 2
                hp = slice(HD * (h % 2), HD * (h % 2) + HD)
                if h >= 2:
                    pe.wait_ge(s_pt, h - 1)
                for sc in range(NCH):
                    mm(bank[h % 2][:, S * sc:S * sc + S], qk[hp, 3 + pt, P * sc:P * sc + P], qk[hp, pt], start=True, stop=True)
                for d in range(2):
                    last = mm(bank[2 + h % 2][:, S * d:S * d + S], cst[0:RH, C_SELM + P * h:C_SELM + P * h + P],
                              row1[0:RH, d], start=True, stop=True)
                last.then_inc(s_mb, 1)
                if h >= 1:
                    weigh(h - 1)
            weigh(RH - 1)

            pe.wait_ge(s_grp, 1)
            for g in range(4):
                for k in range(2):
                    for c in range(NCH):
                        last = tr(pview(g, 0, 2, S)[:, k, P * c:P * c + P],
                                  grp[:, c, P * (2 * g + k):P * (2 * g + k + 1)], ident)
                last.then_inc(s_gT, 1)
            pe.wait_ge(s_gTe, 4)
            pe.wait_ge(s_wout, 32)
            for c in range(NCH):
                for hf in range(2):
                    for k in range(KD):
                        last = mm(bank[4 + 2 * c + hf][:, :], xT[:, k, P * c:P * c + P], wout[hf][:, k],
                                  start=(k == 0), stop=(k == KD - 1))
                    last.then_inc(s_mix, 1)
            for c in range(NCH):
                pe.wait_ge(s_x1, c + 1)
                for q in range(2):
                    for k in range(4):
                        last = tr(pview(2 * c + q, 0, 4, P)[:, k], x_tok[:, c, P * (4 * q + k):P * (4 * q + k + 1)], ident)
                    last.then_inc(s_x1t, 1)
            pe.wait_ge(s_x1e, 4)
            pe.wait_ge(s_late, 16 * 8)
            for c in range(NCH):
                for k in range(KD):
                    last = mm(bank[4][:, NE * c:NE * c + NE], xT[:, k, P * c:P * c + P], rw[:, k], start=(k == 0), stop=(k == KD - 1))
            last.then_inc(s_lg, 1)
            pe.wait_ge(s_msk, 1)
            mm(bank[5][:, 0:NE], tri(0, 0), msk[:, 0], start=True, stop=True)
            mm(bank[5][:, NE:2 * NE], ones, msk[:, 0], start=True, stop=False)
            mm(bank[5][:, NE:2 * NE], tri(0, 0), msk[:, 1], start=False, stop=True)
            mm(bank[5][:, 2 * NE:3 * NE], ones, msk[:, 0], start=True, stop=False)
            mm(bank[5][:, 2 * NE:3 * NE], ones, msk[:, 1], start=False, stop=True).then_inc(s_pos, 1)
            pe.wait_ge(s_moe, 1)
            for c in range(NCH):
                last = tr(bank[6][0:NE, P * c:P * c + P], gates[:, c], ident)
            last.then_inc(s_gtt, 1)
            pe.wait_ge(s_gte, 1)
            for c in range(NCH):
                for hf in range(2):
                    mm(bank[2 * c + hf][:, :], gatesT[0:NE, P * c:P * c + P], b2[0:NE, 512 * hf:512 * hf + 512],
                       start=True, stop=False, skip_group_check=True)

            def gather_rows():
                for c in range(NCH):
                    for hf in range(2):
                        last = mm(bank[7][SLOTS * hf:SLOTS * hf + SLOTS, :], sel[:, c], x_tok[:, c, 512 * hf:512 * hf + 512],
                                  start=(c == 0), stop=(c == NCH - 1))
                last.then_inc(s_gath, 1)

            def gather_turn(n):
                pe.wait_ge(s_xsr, n)
                for j in range(4):
                    last = tr(pview(7, 0, 4, P)[:, j], xsr[:, P * j:P * j + P], ident)
                last.then_inc(s_gtr2, 1)

            def combine(stop):
                for c in range(NCH):
                    for hf in range(2):
                        hp = slice(SLOTS * hf, SLOTS * hf + SLOTS)
                        last = mm(bank[2 * c + hf][:, :], gT[hp, P * c:P * c + P], ysb[hp, :], start=False, stop=stop,
                                  skip_group_check=True)
                return last

            pe.wait_ge(s_sel, 1)
            gather_rows()
            gather_turn(1)
            pe.wait_ge(s_zero, 1)
            pe.wait_ge(s_moe, 2)
            npass = pe.value_load(npass_i[0:1, 0:1], min_val=1, max_val=MAXPASS)
            with pe.Fori(0, npass) as p:
                with pe.Fori(0, NE) as e:
                    it = p * NE + e
                    pe.wait_ge(s_xs, it + 1)
                    for g in range(2):
                        for hf in range(2):
                            hp = slice(SLOTS * hf, SLOTS * hf + SLOTS)
                            mm(bank[4 + g][hp, :], esel[0:NE], b1[0:NE, F * g + 512 * hf:F * g + 512 * hf + 512],
                               start=True, stop=False)
                    for q in range(4):
                        pe.wait_ge(s_slot[q], it * 16 + 16)
                        for k in (2 * q, 2 * q + 1):
                            lhs = xs[:, k % 4, SLOTS * (k // 4):SLOTS * (k // 4) + SLOTS]
                            for g in range(2):
                                for hf in range(2):
                                    hp = slice(SLOTS * hf, SLOTS * hf + SLOTS)
                                    o = F * g + 512 * hf
                                    last = mm(bank[4 + g][hp, :], lhs, w1s[q][:, k % 2, o:o + 512], start=False,
                                              stop=(k == KD - 1))
                        last.then_inc(s_w1, 1)
                        if q == 0:
                            pe.wait_ge(s_yev, it + 1)
                            combine(False)
                        if q == 1:
                            pe.wait_ge(s_gsel, it + 1)
                            for c in range(NCH):
                                last = tr(bank[6][:, P * c:P * c + P], gsel[:, c], ident)
                            last.then_inc(s_gts, 1)
                        if q == 2:
                            pe.wait_ge(s_sel, it + 2)
                            gather_rows()
                    gather_turn(it + 2)
                    pe.wait_ge(s_ht, it + 1)
                    for j in range(4):
                        last = tr(pview(4, 0, 4, P)[:, j], hr[:, P * j:P * j + P], ident)
                    last.then_inc(s_htr, 1)
                    pe.wait_ge(s_htev, it + 1)
                    pe.wait_ge(s_gtev, it + 1)
                    for k in range(KD):
                        if k % 4 == 0:
                            pe.wait_ge(s_slot[4 + k // 4], it * 16 + 16)
                        for hf in range(2):
                            last = mm(bank[6][SLOTS * hf:SLOTS * hf + SLOTS, :],
                                      hT[:, k % 4, SLOTS * (k // 4):SLOTS * (k // 4) + SLOTS],
                                      w2s[k // 4][:, k % 4, 512 * hf:512 * hf + 512], start=(k == 0), stop=(k == KD - 1))
                        if k % 4 == 3:
                            last.then_inc(s_w2, 1)
            pe.wait_ge(s_yev, npass * NE + 1)
            combine(True).then_inc(s_all, 1)

        @block.gpsimd
        def _(pool):
            nc.gpsimd.memset(mv[:, :, :, HD:HD + 1], 1.0).then_inc(s_one, 1)
            for pt in range(NP):
                for d in range(2):
                    pool.wait_ge(s_prev, 4 * pt + 2 * d + 2)
                    m = mpT[:, d, :, 0:P]
                    nc.gpsimd.tensor_tensor(m, m, ident.unsqueeze(1).broadcast_to([P, 4, P]), ALU.add).then_inc(s_pch, 1)
                    pool.wait_ge(s_pch, 2 * pt + d + 1)
                    x2 = cst[:, C_X2 + P * d:C_X2 + P * d + P]
                    nc.gpsimd.tensor_tensor(xmT[:, d], m, x2.unsqueeze(1).broadcast_to([P, 4, P]), ALU.mult).then_inc(s_gps, 1)
            for h in range(RH):
                pool.wait_ge(s_de, h + 1)
                for d in range(2):
                    diag = ebuf_[h % 2][:, d].rearrange("p (b t) -> p b t", b=3)[:, 0::2]
                    last = nc.gpsimd.tensor_tensor(diag, diag, tri(d, 1).unsqueeze(1).broadcast_to([P, 2, P]), ALU.mult)
                last.then_inc(s_dm, 1)
            pool.wait_ge(s_grp, 1)
            for i, name in enumerate(("ln1_g", "ln1_b", "ln2_g", "ln2_b")):
                pool.dma_start(ln4[:, i], row_bc(t[name][0])).then_inc(s_late, 16)
            pool.dma_start(rw, t["router_w"][0].rearrange("(k p) e -> p k e", p=P)).then_inc(s_late, 16)
            pool.dma_start(rb, row_bc(t["router_b"][0])).then_inc(s_late, 16)
            pool.dma_start(b2[0:NE], t["exp_b2"][0]).then_inc(s_late, 16)
            pool.dma_start(b1[0:NE], t["exp_b1"][0]).then_inc(s_late, 16)
            nc.gpsimd.memset(gT, 0.0).then_inc(s_zero, 1)
            nc.gpsimd.memset(ysb, 0.0).then_inc(s_yev, 1)
            pool.wait_ge(s_late, 16 * 8)

        @block.vector
        def _(dve):
            steps = [0]
            norms = [0]
            V = nc.vector

            def link(ins):
                steps[0] += 1
                ins.then_inc(s_dch, 1)
                dve.wait_ge(s_dch, steps[0])

            def norm(a, tmp, g, w, eps):
                link(V.tensor_reduce(st1[:, 0:g], a, X, ALU.add))
                link(V.tensor_scalar(st1[:, 0:g], st1[:, 0:g], 1.0 / w, None, ALU.mult))
                link(V.tensor_tensor(a, a, spread(st1[:, 0:g], w), ALU.subtract))
                link(V.tensor_tensor(tmp, a, a, ALU.mult))
                link(V.tensor_reduce(st2[:, 0:g], tmp, X, ALU.add))
                norms[0] += 1
                V.tensor_scalar(st2[:, 0:g], st2[:, 0:g], 1.0 / w, eps, ALU.mult, ALU.add).then_inc(s_var, 1)
                dve.wait_ge(s_std, norms[0])
                link(V.reciprocal(st2[:, 0:g], st2[:, 0:g]))
                link(V.tensor_tensor(a, a, spread(st2[:, 0:g], w), ALU.mult))

            def wide(a, n):
                return a.unsqueeze(1).broadcast_to([P, n] + list(a.shape[1:]))

            dve.wait_ge(s_ptr, 1)
            V.tensor_copy(wsT, pview(5, 0, 4, P))
            link(V.tensor_copy(pcol, bank[4][:, 0:NROWS]))
            V.memset(st1, 0.0).then_inc(s_pev, 1)
            m0, m1 = pcol[:, ROWS["mu0"]:ROWS["mu0"] + 11], pcol[:, ROWS["mu1"]:ROWS["mu1"] + 11]
            link(V.scalar_tensor_tensor(own, m0, -1.0, m1, ALU.mult, ALU.subtract))
            V.tensor_scalar(own, own, 1.0, None, ALU.add).then_inc(s_pev, 1)

            def shifted(i):
                dve.wait_ge(s_base, i + 1)
                _, _, kind, j = T_TILES[i]
                src, b = bank[i % 4], base[:, i % 2]
                if i < NR:
                    m = MU_COL[kind] + (j if kind in "rkv" else 0)
                    prev, nxt = par("mu0", m), par("mu1", m)
                    dst = {"r": rT, "k": kT, "v": vT}[kind][:, j] if kind in "rkv" else {"wa": wa, "gd": gd}[kind]
                else:
                    prev, nxt = par("cw", j), par("cw", 12 + j)
                    dst = qk[:, j]
                link(V.scalar_tensor_tensor(b[:, 1:S], src[:, 0:S - 1], prev, b[:, 1:S], ALU.mult, ALU.add))
                V.scalar_tensor_tensor(dst[:, 0:S - 1], src[:, 1:S], nxt, b[:, 0:S - 1], ALU.mult, ALU.add)
                V.tensor_copy(dst[:, S - 1:S], b[:, S - 1:S]).then_inc(s_shift, 1)

            for i in range(NR):
                shifted(i)
            dve.wait_ge(s_shift, NR)
            for j in range(NP):
                last = V.tensor_scalar(kkraw[:, j], kT[:, j], par("kk", j), None, ALU.mult)
            link(last)
            V.tensor_tensor(kksq, kkraw, kkraw, ALU.mult).then_inc(s_sq, 1)
            shifted(11)
            shifted(12)
            dve.wait_ge(s_ss, 1)
            kkf = kk.rearrange("p a s -> p (a s)")
            V.tensor_scalar(kkf[:, 0:512], bank[6][:, :], 1e-24, None, ALU.max).then_inc(s_kmx, 1)
            V.tensor_scalar(kkf[:, 512:768], bank[7][:, 0:S], 1e-24, None, ALU.max).then_inc(s_kmx, 1)
            for i in range(13, NT):
                shifted(i)
            dve.wait_ge(s_kkd, 1)
            link(V.reciprocal(kk, kk))
            link(V.tensor_tensor(kk, kk, kkraw, ALU.mult))

            def prep_scan(pt):
                dve.wait_ge(s_sig, pt + 1)
                for d in range(2):
                    for c in range(NCH):
                        o = srel[:, d, P * c:P * c + P]
                        i = sigw[:, pt, d, P * c:P * c + P]
                        if d:
                            o, i = o[:, ::-1], i[:, ::-1]
                        last = V.tensor_tensor_scan(o, ones, i, 0.0, ALU.mult, ALU.add)
                link(last)

            def prep_relative(pt):
                s4 = srel.rearrange("p d (c t) -> p d c t", c=NCH)
                V.tensor_scalar(sref[:, 0], s4[:, 0, :, P - 1], 0.5, None, ALU.mult)
                link(V.tensor_scalar(sref[:, 1], s4[:, 1, :, 0], 0.5, None, ALU.mult))
                V.tensor_tensor(gam[:, pt % 2], sref[:, :, 0], sref[:, :, 1], ALU.add)
                sf = srel.rearrange("p d (c t) -> p (d c) t", c=NCH)
                link(V.tensor_tensor(sf, sf, spread(sref.rearrange("p d c -> p (d c)"), P), ALU.subtract))
                V.tensor_tensor(s_exc, srel, sigw[:, pt], ALU.subtract).then_inc(s_rel, 1)

            def prep_keys(pt):
                V.tensor_scalar(rrk, rT[:, pt], par("rk", pt), None, ALU.mult)
                link(V.tensor_scalar(kka, kT[:, pt], par("ka", pt), None, ALU.mult))
                link(V.scalar_tensor_tensor(tmpk, icl[:, pt], -1.0, wide(kka, 2), ALU.add, ALU.mult))
                link(V.tensor_tensor(kdir, tmpk, wide(kT[:, pt], 2), ALU.add))
                link(V.tensor_tensor(kds, kdir[:, 0], kdir[:, 1], ALU.add))
                V.tensor_tensor(bon[:, pt], rrk, kds, ALU.mult).then_inc(s_bon, 1)
                link(V.tensor_tensor(tmpk, icl[:, pt], wide(kk[:, pt], 2), ALU.mult))

            def prep_operands(pt):
                ar, kt, bt = ar_[pt % 2], kt_[pt % 2], bt_[pt % 2]
                dve.wait_ge(s_exp, pt + 1)

                def by_chunk(a):
                    return a.rearrange("p d (c t) -> p d c t", c=NCH)

                V.tensor_tensor(kt, by_chunk(kdir), by_chunk(e_inv), ALU.mult)
                V.tensor_tensor(bt, by_chunk(tmpk), by_chunk(e_inv), ALU.mult)
                for d in range(2):
                    V.scalar_tensor_tensor(ar[:, d, :, 0], by_chunk(s_exc)[:, d], -1.0,
                                           kk[:, pt].rearrange("p (c t) -> p c t", c=NCH), ALU.mult, ALU.mult)
                    last = V.tensor_tensor(ar[:, d, :, 1], by_chunk(e_inc)[:, d],
                                           rT[:, pt].rearrange("p (c t) -> p c t", c=NCH), ALU.mult)
                last.then_inc(s_ops, 1)

            prep_scan(0)
            prep_relative(0)
            prep_keys(0)
            dve.wait_ge(s_silu, 1)
            V.tensor_tensor(qk[:, 0:3], qk[:, 0:3], sgq[:, 0:3], ALU.mult)
            V.scalar_tensor_tensor(qk[:, 3:6], sgq[:, 3:6], HD ** -0.5, qk[:, 3:6], ALU.mult, ALU.mult).then_inc(s_qk, 1)
            prep_operands(0)
            dve.wait_ge(s_gtr, 1)
            dve.wait_ge(s_small, 64)
            r0, r1, r2, r3 = row0[0:RH], row1[0:RH], row2[0:RH], row3[0:RH]
            for d in range(2):
                V.tensor_scalar(r3[:, d], bank[4][0:RH, S * d:S * d + S], gbias[0:RH, d:d + 1], None, ALU.add)
                last = V.tensor_scalar(r0[:, d], bank[5][0:RH, S * d:S * d + S], gbias[0:RH, 2 + d:3 + d], None, ALU.add)
            link(last)
            V.scalar_tensor_tensor(r1, r0, -1.0, r0, ALU.mult, ALU.max).then_inc(s_grow, 1)

            def gate_rows():
                dve.wait_ge(s_gact, 1)
                link(V.scalar_tensor_tensor(r0, r0, 0.0, r1, ALU.min, ALU.subtract))
                for d in range(2):
                    a, b = r0[:, d], r2[:, d]
                    if d:
                        a, b = a[:, ::-1], b[:, ::-1]
                    on = ones[0:RH, 0:1].broadcast_to([RH, S])
                    last = V.tensor_tensor_scan(b, on, a, 0.0, ALU.mult, ALU.add)
                link(last)
                link(V.tensor_tensor(r3, r3, r2, ALU.subtract))
                for d in range(2):
                    a, b = r3[:, d], r1[:, d]
                    if d:
                        a, b = a[:, ::-1], b[:, ::-1]
                    last = V.tensor_tensor_scan(b, a, a, 0.0, ALU.max, ALU.max)
                link(last)
                V.tensor_tensor(r0, r1, r2, ALU.add).then_inc(s_grow, 1)

            def gmlp_norm():
                dve.wait_ge(s_base, NT + 6)
                dve.wait_ge(s_lnb, 80)
                v = gel[:, :, GW:2 * GW]
                norm(v, kkraw.rearrange("p a s -> p (a s)")[:, 0:512].rearrange("p (c w) -> p c w", c=2), 2, GW, LN_EPS)
                link(V.tensor_tensor(v, v, wide(lnb[:, 0:GW], 2), ALU.mult))
                V.tensor_tensor(v, v, wide(lnb[:, GW:2 * GW], 2), ALU.add).then_inc(s_gv, 1)

            for pt in range(NP):
                for d in range(2):
                    for kind, b, dst in ((0, 4 * d, nqT), (1, 4 * d + 2, mpT)):
                        dve.wait_ge(s_prod, 4 * pt + 2 * d + kind + 1)
                        for half in range(2):
                            last = V.tensor_tensor(dst[:, d, 2 * half:2 * half + 2], pview(b + half, 0, 2, 256),
                                                   wide(mask2(d), 2), ALU.mult)
                        last.then_inc(s_prev, 1)
                for n in range(len(LEVELS)):
                    for d in range(2):
                        dve.wait_ge(s_a, 12 * pt + 2 * n + d + 1)
                        V.tensor_tensor(gm[:, d], pview(4 * d, 0, 4, P), wide(gmask(d, n), 4), ALU.mult).then_inc(s_g, 1)
                    if pt + 1 < NP:
                        if n == 0:
                            prep_scan(pt + 1)
                        if n == 1:
                            prep_relative(pt + 1)
                        if n == 2:
                            prep_keys(pt + 1)
                        if n == 5:
                            prep_operands(pt + 1)
                    else:
                        if n == 0:
                            gate_rows()
                        if n == 2:
                            gmlp_norm()
                for step in range(2):
                    for d in range(2):
                        cw = d if step == 0 else 1 - d
                        dve.wait_ge(s_w, 4 * pt + 2 * step + d + 1)
                        for h in range(2):
                            last = V.tensor_copy(wbuf[:, d, 2 * h + cw], bank[4 * d + 3 * (1 - h)][:, 192:192 + HD])
                        last.then_inc(s_wev, 1)
                for c in range(NCH):
                    dve.wait_ge(s_o, 2 * pt + c + 1)
                    for h in range(2):
                        last = V.tensor_copy(orw[:, c, 2 * pt + h], bank[1 + 4 * c + h][:, 0:HD])
                    last.then_inc(s_oev, 1)

            dve.wait_ge(s_gmix, 1)
            for g in range(4):
                V.scalar_tensor_tensor(grp[:, :, HD * g:HD * g + HD], pview(6, P * g, NCH, HD), par("bs", g),
                                       gel[:, :, HD * g:HD * g + HD], ALU.add, ALU.mult)
            dve.wait_ge(s_bs, 1)
            V.tensor_copy(emt, pview(7, 24, 2, NCH, RH)).then_inc(s_gcol, 1)
            link(V.tensor_copy(gcolm, pview(7, 0, 2, NCH, RH)))
            link(V.tensor_copy(bsum, pview(7, 64, NCH, RH)))
            dve.wait_ge(s_oev, 2 * NP)

            def args(h):
                dve.wait_ge(s_mb, h + 1)
                if h >= 2:
                    dve.wait_ge(s_pt, h - 1)
                mb, ebuf = bank[2 + h % 2], ebuf_[h % 2]
                for d, col, sc, t0, n in ((0, 0, 0, 0, S), (0, S, 1, P, P), (1, 0, 0, 0, P), (1, P, 1, 0, S)):
                    last = V.tensor_scalar(ebuf[:, d, col:col + n], mb[:, S * d + t0:S * d + t0 + n],
                                           gcolm[:, d, sc, h:h + 1], 0.0, ALU.subtract, ALU.max)
                last.then_inc(s_arg, 1)

            def weights(h):
                dve.wait_ge(s_dm, h + 1)
                if h:
                    dve.wait_ge(s_pv, h)
                sc_b, ebuf = bank[h % 2], ebuf_[h % 2]
                for d, col, src, n in ((0, 0, 0, S), (0, S, S + P, P), (1, 0, 0, P), (1, P, S, S)):
                    last = V.tensor_tensor(pbuf[:, d, col:col + n], ebuf[:, d, col:col + n], sc_b[:, src:src + n], ALU.mult)
                last.then_inc(s_pt, 1)

            def divide(h):
                dve.wait_ge(s_pv, h + 1)
                if h == 0:
                    dve.wait_ge(s_gcev, 1)
                nd = pview(4 + h % 2, 0, 2, NCH, 65)
                link(V.tensor_scalar(den, nd[:, :, :, HD], -1.0, None, ALU.mult))
                link(V.tensor_tensor(den, den, nd[:, :, :, HD], ALU.max))
                link(V.tensor_tensor(den, den, emt[:, :, :, h], ALU.max))
                link(V.reciprocal(rec, den))
                for d in range(2):
                    last = V.tensor_tensor(ntmp[:, d], nd[:, d, :, 0:HD], spread(rec[:, d], HD), ALU.mult)
                link(last)
                V.tensor_tensor(hm[:, :, h], ntmp[:, 0], ntmp[:, 1], ALU.add).then_inc(s_hn, 1)

            args(0)
            for h in range(RH):
                if h + 1 < RH:
                    args(h + 1)
                weights(h)
                if h:
                    divide(h - 1)
            divide(RH - 1)
            dve.wait_ge(s_hn, RH)

            def flat(a):
                return a.rearrange("p c h e -> p (c h) e")

            ta = view(o_m, NCH * RH, HD)
            norm(flat(hm), ta, NCH * RH, HD, LN_EPS)
            hm2 = hm.rearrange("p c h e -> p c (h e)")
            ro, n = LNO["mg"]
            link(V.tensor_tensor(hm2, hm2, wide(lnb[:, ro:ro + n], 2), ALU.mult))
            V.tensor_tensor(grp[:, :, GW + RW:D], hm2, osig, ALU.mult)
            norm(flat(orw), ta, NCH * RH, HD, GN_EPS)
            o2 = orw.rearrange("p c h e -> p c (h e)")
            ro, n = LNO["rg"]
            link(V.tensor_tensor(o2, o2, wide(lnb[:, ro:ro + n], 2), ALU.mult))
            ro, n = LNO["rb"]
            link(V.tensor_tensor(o2, o2, wide(lnb[:, ro:ro + n], 2), ALU.add))
            link(V.tensor_tensor(ta, vtok.rearrange("p c (h e) -> p (c h) e", h=RH),
                                 spread(bsum.rearrange("p c h -> p (c h)"), HD), ALU.mult))
            link(V.tensor_tensor(o2, o2, ta.rearrange("p (c h) e -> p c (h e)", c=NCH), ALU.add))
            V.tensor_tensor(grp[:, :, GW:GW + RW], o2, gate_r, ALU.mult).then_inc(s_grp, 1)

            def layer_norm(c, which):
                a = x_tok[:, c:c + 1]
                norm(a, lnt[:, c:c + 1], 1, D, LN_EPS)
                link(V.tensor_tensor(a, a, ln4[:, 2 * which:2 * which + 1], ALU.mult))
                return V.tensor_tensor(a, a, ln4[:, 2 * which + 1:2 * which + 2], ALU.add)

            dve.wait_ge(s_late, 16 * 8)
            for c in range(NCH):
                dve.wait_ge(s_mix, 2 * c + 2)
                for hf in range(2):
                    xh = x_tok[:, c, 512 * hf:512 * hf + 512]
                    last = V.scalar_tensor_tensor(xh, xh, ALPHA, bank[4 + 2 * c + hf][:, :], ALU.mult, ALU.add)
                link(last)
                layer_norm(c, 0).then_inc(s_x1, 1)

            dve.wait_ge(s_lg, 1)
            link(V.tensor_tensor(lg, pview(4, 0, NCH, NE), wide(rb, NCH), ALU.add))
            for c in range(NCH):
                last = V.max(mx[:, c], lg[:, c])
            link(last)
            v4 = mx[:, :, TOPK - 1:TOPK].broadcast_to([P, NCH, NE])
            V.tensor_scalar(small[:, 0:2], mx[:, :, 0], -1.0, None, ALU.mult).then_inc(s_rexp_in, 1)
            V.tensor_tensor(mgt, lg, v4, ALU.is_gt)
            link(V.tensor_tensor(meq, lg, v4, ALU.is_equal))
            V.tensor_reduce(small[:, 4:6], mgt, X, ALU.add)
            for c in range(NCH):
                last = V.tensor_tensor_scan(mcum[:, c], ones[:, 0:NE], meq[:, c], 0.0, ALU.mult, ALU.add)
            link(last)
            link(V.tensor_scalar(small[:, 4:6], small[:, 4:6], -1.0, float(TOPK), ALU.mult, ALU.add))
            link(V.tensor_tensor(mcum, mcum, spread(small[:, 4:6], NE), ALU.is_le))
            link(V.tensor_tensor(meq, meq, mcum, ALU.mult))
            V.tensor_tensor(msk, mgt, meq, ALU.add).then_inc(s_msk, 1)
            dve.wait_ge(s_msk, 1)
            dve.wait_ge(s_rexp, 1)
            link(V.tensor_tensor(gates, gates, msk, ALU.mult))
            link(V.tensor_reduce(small[:, 8:10], gates, X, ALU.add))
            link(V.reciprocal(small[:, 8:10], small[:, 8:10]))
            link(V.tensor_tensor(gates, gates, spread(small[:, 8:10], NE), ALU.mult))
            dve.wait_ge(s_pos, 1)
            link(V.scalar_tensor_tensor(mcum, pview(5, 0, NCH, NE), 1.0, msk, ALU.add, ALU.mult))
            for i in range(MAXPASS):
                V.tensor_scalar(posm[:, :, NE * i:NE * i + NE], mcum, -1.0 - SLOTS * i, None, ALU.add)
                V.tensor_copy(gatex[:, :, NE * i:NE * i + NE], gates)
            V.memset(posm[:, :, NE * MAXPASS:], -1.0)
            link(V.memset(gatex[:, :, NE * MAXPASS:], 0.0))
            V.tensor_reduce(small[:, 12:13], bank[5][:, 2 * NE:3 * NE], X, ALU.max).then_inc(s_moe, 1)
            dve.wait_ge(s_moe, 1)
            link(V.tensor_scalar(small[:, 16:17], small[:, 12:13], float(SLOTS), None, ALU.is_gt))
            for i in range(2, MAXPASS):
                link(V.scalar_tensor_tensor(small[:, 16:17], small[:, 12:13], float(SLOTS * i), small[:, 16:17],
                                            ALU.is_gt, ALU.add))
            V.tensor_scalar(npass_i[:, :], small[:, 16:17], 1.0, None, ALU.add).then_inc(s_moe, 1)
            iota = cst[:, C_IOTA:C_IOTA + P]
            for i in range(MAXPASS):
                V.tensor_copy(hot[0:NE, NE * i:NE * i + NE], ident[0:NE, 0:NE])
            link(V.memset(hot[0:NE, NE * MAXPASS:], 0.0))

            for c in range(NCH):
                last = V.tensor_scalar(sel[:, c], iota[:, 0:SLOTS], posm[:, c, 0:1], None, ALU.is_equal)
            V.tensor_scalar(esel[0:NE], ones[0:NE, 0:SLOTS], hot[0:NE, 0:1], None, ALU.mult).then_inc(s_sel, 1)
            dve.wait_ge(s_moe, 2)
            npass = dve.value_load(npass_i[0:1, 0:1], min_val=1, max_val=MAXPASS)
            with dve.Fori(0, npass) as p:
                with dve.Fori(0, NE) as e:
                    it = p * NE + e
                    dve.wait_ge(s_w1, it * 4 + 1)
                    for c in range(NCH):
                        last = V.tensor_scalar(gsel[:, c], iota, posm[:, c, bass.ds(it, 1)],
                                               gatex[:, c, bass.ds(it, 1)], ALU.is_equal, ALU.mult)
                    last.then_inc(s_gsel, 1)
                    for c in range(NCH):
                        V.tensor_scalar(sel[:, c], iota[:, 0:SLOTS], posm[:, c, bass.ds(it + 1, 1)], None, ALU.is_equal)
                    V.tensor_scalar(esel[0:NE], ones[0:NE, 0:SLOTS], hot[0:NE, bass.ds(it + 1, 1)], None,
                                    ALU.mult).then_inc(s_sel, 1)
                    dve.wait_ge(s_w1, it * 4 + 4)
                    V.tensor_scalar(hr, bank[4][:, :], 7.0, None, ALU.min).then_inc(s_hg, 1)
                    V.tensor_scalar(ur, bank[5][:, :], 7.0, -7.0, ALU.min, ALU.max).then_inc(s_hu, 1)
                    dve.wait_ge(s_hs, it + 1)
                    V.tensor_tensor(hr, hr, sg, ALU.mult).then_inc(s_hm, 1)
                    dve.wait_ge(s_hu, it + 1)
                    dve.wait_ge(s_hm, it + 1)
                    V.scalar_tensor_tensor(hr, ur, 1.0, hr, ALU.add, ALU.mult).then_inc(s_ht, 1)
            dve.wait_ge(s_all, 1)
            for c in range(NCH):
                for hf in range(2):
                    xh = x_tok[:, c, 512 * hf:512 * hf + 512]
                    last = V.scalar_tensor_tensor(xh, xh, ALPHA, bank[2 * c + hf][:, :], ALU.mult, ALU.add)
                last.then_inc(s_x2r, 1)
                dve.wait_ge(s_x2r, c + 1)
                layer_norm(c, 1).then_inc(s_fin, 1)


_INS = ["x", "w_in", "gmlp_ln_g", "gmlp_ln_b", "gmlp_ws", "gmlp_bs", "rwkv_mu", "rwkv_w0", "rwkv_w2", "rwkv_a0",
        "rwkv_a2", "rwkv_g2", "rwkv_k_k", "rwkv_k_a", "rwkv_r_k", "rwkv_ln_g", "rwkv_ln_b", "mlstm_conv_w",
        "mlstm_conv_b", "mlstm_gate_b", "mlstm_ln_g", "w_out", "ln1_g", "ln1_b", "router_w", "router_b",
        "exp_w1", "exp_b1", "exp_w2", "exp_b2", "ln2_g", "ln2_b"]
DEBUG = False


def kernel(**inputs):
    import concourse.bacc as bacc
    from concourse.bass_utils import run_bass_kernel_spmd

    nc = bacc.Bacc("TRN2", target_bir_lowering=False, num_devices=1)
    f32 = mybir.dt.float32
    arrays, t = {}, {}
    for name in _INS:
        a = np.ascontiguousarray(inputs[name])
        arrays[f"in_{name}"] = a
        t[name] = nc.dram_tensor(f"in_{name}", a.shape, mybir.dt.from_np(a.dtype), kind="ExternalInput").ap()
    arrays["in_consts"] = constants()
    t["consts"] = nc.dram_tensor("in_consts", (P, NCONST), f32, kind="ExternalInput").ap()
    out = nc.dram_tensor("out", (1, S, D), f32, kind="ExternalOutput").ap()
    dbg = {"grp": nc.dram_tensor("dbg_grp", (S, D), f32, kind="ExternalOutput").ap()} if DEBUG else None
    encoder_kernel(nc, t, out, dbg)
    r = run_bass_kernel_spmd(nc, [arrays], core_ids=[0])
    return r.results[0]["out"]
```

```python
import numpy as np
import concourse.bass as bass
from concourse import mybir
from contextlib import ExitStack

P = 128
D = 1024
S = 256
KD = D // P
NCH = S // P
HD = 64
RH = 6
RW = RH * HD
NP = RH // 2
GW = 256
NE = 32
TOPK = 4
SLOTS = 64
AHEAD = 8
MAXPASS = S // SLOTS
F = 1024
R0 = 512
M0 = R0 + 3 * RW + 256
PIN = M0 + 4 * RW + 24
LEVELS = (2, 4, 8, 16, 32, 64)
KAPPA = float(np.exp(-0.5))
ALPHA = 2.0 ** 0.25
LN_EPS = 1e-5
GN_EPS = 64e-5
BIG = 1e30

C_ID, C_BONE = 0, 128
C_MASK2 = 256
C_GM = C_MASK2 + 512
C_X2 = C_GM + 2 * len(LEVELS) * P
C_HSEL = C_X2 + 2 * P
C_SELM = C_HSEL + 2
C_ONES = C_SELM + RH * P
C_IOTA = C_ONES + P
NCONST = C_IOTA + P


def constants():
    c = np.zeros((P, NCONST), np.float32)
    i = np.arange(P)
    row, col = i[:, None], i[None, :]
    c[:, C_ID:C_ID + P] = row == col
    c[:, C_BONE:C_BONE + P] = row // HD == col // HD
    for d in range(2):
        before = (row < col) if d == 0 else (row > col)
        c[:, C_MASK2 + 256 * d:C_MASK2 + 256 * d + P] = before
        c[:, C_MASK2 + 256 * d + P:C_MASK2 + 256 * d + 256] = before | (row == col)
        late, early = (row, col) if d == 0 else (col, row)
        for n, m in enumerate(LEVELS):
            off = (late // (2 * m) == early // (2 * m)) & (late // m % 2 == 1) & (early // m % 2 == 0)
            o = C_GM + (d * len(LEVELS) + n) * P
            c[:, o:o + P] = off | (row == col)
        late, early = early, late
        off = (late // 2 == early // 2) & (late % 2 == 1) & (early % 2 == 0)
        c[:, C_X2 + d * P:C_X2 + (d + 1) * P] = off | (row == col)
    c[:, C_HSEL:C_HSEL + 2] = row // HD == np.arange(2)[None, :]
    for h in range(RH):
        c[h, C_SELM + h * P:C_SELM + (h + 1) * P] = 1.0
    c[:, C_ONES:C_ONES + P] = 1.0
    c[:, C_IOTA:C_IOTA + P] = np.arange(P)[None, :] % SLOTS
    return c


ROWS = {}
_n = 0
for _name, _k in (("mu0", 11), ("mu1", 11), ("w0", 6), ("a0", 6), ("kk", 3), ("ka", 3), ("rk", 3),
                  ("cw", 18), ("cb", 6), ("bs", 4)):
    ROWS[_name] = _n
    _n += _k
NROWS = _n

T_TILES = ([("C", 0, "v", 2), ("C", 128, "wa", 0), ("C", 256, "gd", 0)]
           + [("A", 128 * i, "rk"[i // 3], i % 3) for i in range(4)]
           + [("B", 0, "k", 1), ("B", 128, "k", 2), ("B", 256, "v", 0), ("B", 384, "v", 1)]
           + [("D", 128 * i, "m", i) for i in range(4)] + [("E", 0, "m", 4), ("E", 128, "m", 5)])
MU_COL = {"r": 0, "k": 3, "v": 6, "wa": 9, "gd": 10}
NR = 11
NT = len(T_TILES)
PIECES = {"C": (R0 + 1024, 384, 2), "A": (R0, 512, 3), "B": (R0 + 512, 512, 4), "D": (M0, 512, 5),
          "E": (M0 + 512, 256, 0), "F": (M0 + 768, 384, 1), "G": (M0 + 1152, 408, 0), "H": (0, 512, 1)}
FILLS = ((0, 2, 0), (0, 3, 1), (1, 2, 0), (1, 3, 1), (0, 0, 2), (0, 1, 0), (1, 0, 2), (1, 1, 0))
OUT_ORDER = ((0, 1), (5, 6), (7, 2), (3, 4))
TOK_TILES = [(p, c) for p in "FGH" for c in range(NCH)]


def encoder_kernel(nc, t, out, dbg=None):
    f32 = mybir.dt.float32
    i32 = mybir.dt.int32
    ALU = mybir.AluOpType
    ACT = mybir.ActivationFunctionType
    X = mybir.AxisListType.X
    ctx = ExitStack()
    with ctx:
        def sem(name):
            return ctx.enter_context(nc.semaphore(name))

        SLOT = 4096
        ring = ctx.enter_context(nc.sbuf_tensor("ring", [P, 6 * SLOT], f32))
        POOLN = 28620
        pool_t = ctx.enter_context(nc.sbuf_tensor("pool", [P, POOLN], f32))
        bank = [ctx.enter_context(nc.psum_tensor(f"bank{i}", [P, 512], f32)) for i in range(8)]
        npass_i = ctx.enter_context(nc.sbuf_tensor("npass_i", [P, 1], i32))

        top = [0]

        def carve(n):
            o = top[0]
            top[0] += n
            assert top[0] <= POOLN, top[0]
            return o

        def view(o, *shape):
            n = int(np.prod(shape))
            a = pool_t[:, o:o + n]
            names = "abcd"[:len(shape)]
            if len(shape) == 1:
                return a
            return a.rearrange(f"p ({' '.join(names)}) -> p {' '.join(names)}",
                               **{k: v for k, v in zip(names[1:], shape[1:])})

        def rview(slot, o, *shape):
            n = int(np.prod(shape))
            a = ring[:, slot * SLOT + o:slot * SLOT + o + n]
            names = "abcd"[:len(shape)]
            if len(shape) == 1:
                return a
            return a.rearrange(f"p ({' '.join(names)}) -> p {' '.join(names)}",
                               **{k: v for k, v in zip(names[1:], shape[1:])})

        def pview(b, o, *shape):
            n = int(np.prod(shape))
            a = bank[b][:, o:o + n]
            names = "abcd"[:len(shape)]
            if len(shape) == 1:
                return a
            return a.rearrange(f"p ({' '.join(names)}) -> p {' '.join(names)}",
                               **{k: v for k, v in zip(names[1:], shape[1:])})

        def spread(a, n):
            return a.unsqueeze(len(a.shape)).broadcast_to(list(a.shape) + [n])

        cst = view(carve(NCONST), NCONST)
        x_tok = view(carve(2048), NCH, D)
        o_xT = carve(2048)
        xT = view(o_xT, KD, S)
        o_grp = carve(2048)
        grp = view(o_grp, NCH, D)
        pcol = view(carve(NROWS), NROWS)
        o_s = carve(1536)
        sigw = view(o_s, NP, 2, S)
        icl = view(carve(1536), NP, 2, S)
        o_kk = carve(768)
        kk = view(o_kk, NP, S)
        bon = view(carve(768), NP, S)
        o_m = top[0]
        rT = view(carve(768), NP, S)
        kT = view(carve(768), NP, S)
        o_vT = carve(768)
        vT = view(o_vT, NP, S)
        o_wa = carve(S)
        wa = view(o_wa, S)
        gd = view(carve(S), S)
        base = view(carve(2 * S), 2, S)
        wbuf = view(carve(512), 2, 4, HD)
        ubuf = view(carve(512), 2, 4, HD)
        hst = view(carve(2 * P), 2, P)
        vtok = view(carve(NCH * RW), NCH, RW)
        gate_r = view(carve(NCH * RW), NCH, RW)
        qk = view(carve(6 * S), 6, S)
        mv = view(carve(NCH * RH * 65), NCH, RH, 65)
        gel = view(carve(1024), NCH, 512)
        gt = view(carve(NCH * 24), NCH, 24)
        lnb = view(carve(2 * GW + 3 * RW), 2 * GW + 3 * RW)
        o_lora = carve(2 * RW)
        lora2 = view(o_lora, 2, RW)
        osig = view(o_lora, NCH, RW)
        g2 = view(carve(RW), RW)
        wsT = view(carve(512), 4, P)
        gbias = view(carve(4), 4)
        stat = {k: (view(carve(4), 4), view(carve(4), 4)) for k in ("r", "m", "g")}
        ebuf = view(o_wa, 2, 384)
        pbuf = view(carve(768), 2, 384)
        sq = rview(4, 3840, NCH * 2, HD)
        gcolm = view(carve(2 * NCH * RH), 2, NCH, RH)
        emt = view(carve(NCH * RH * 2), 2, NCH, RH)
        gam = view(carve(4), 2, 2)
        own = view(carve(11), 11)
        sref = view(carve(4), 2, NCH)
        den = view(carve(4), 2, NCH)
        rec = view(carve(4), 2, NCH)
        bsum = view(carve(NCH * RH), NCH, RH)
        mix_top = top[0]
        sgq = view(o_grp, 6, S)
        kkraw = rview(4, 0, NP, S)
        kksq = rview(4, 768, NP, S)
        orw = view(o_vT, NCH, 2, HD)
        hm = view(o_vT + 256, NCH, 2, HD)
        ntmp = view(o_vT + 512, 2, NCH, HD)
        row0 = view(o_xT, 2, S)
        row1 = view(o_xT + 512, 2, S)
        row2 = view(o_xT + 1024, 2, S)
        row3 = view(o_xT + 1536, 2, S)
        prow = view(o_grp, P)
        wsraw = view(o_grp + 128, 4, P)
        nqT = rview(2, 0, 2, 4, 256)
        mpT = rview(2, 2048, 2, 4, 256)
        xm = rview(3, 0, 2, 4, P)
        oT = rview(3, 3584, NCH, P)
        xmT = rview(3, 1024, 2, 4, P)
        gm = rview(3, 2048, 2, 4, P)
        bktok = rview(3, 3072, 2, 2, P)
        srel = rview(4, 0, 2, S)
        s_exc = rview(4, 512, 2, S)
        e_inc = rview(4, 1024, 2, S)
        gsq = rview(3, 3584, NCH, GW)
        e_inv = rview(4, 1536, 2, S)
        kdir = rview(4, 2048, 2, S)
        tmpk = rview(4, 2560, 2, S)
        rrk = rview(4, 3072, S)
        kka = rview(4, 3328, S)
        kds = rview(4, 3584, S)
        ar_ = [rview(5, 1024 * b, 2, NCH, 2, P) for b in range(2)]
        ktz = [rview(5, 2048 + 512 * h, 2, NCH, P) for h in range(2)]
        btz = [rview(5, 3072 + 512 * h, 2, NCH, P) for h in range(2)]
        wout = [rview(h, 0, KD, 512) for h in range(2)]
        ln4 = view(o_s, 4, D)
        top[0] = o_m
        rw = view(carve(KD * NE), KD, NE)
        rb = view(carve(NE), NE)
        b2 = view(carve(D), D)
        lg = view(carve(NCH * NE), NCH, NE)
        mx = view(carve(NCH * 8), NCH, 8)
        mgt = view(carve(NCH * NE), NCH, NE)
        meq = view(carve(NCH * NE), NCH, NE)
        mcum = view(carve(NCH * NE), NCH, NE)
        msk = view(carve(NCH * NE), NCH, NE)
        gates = view(carve(NCH * NE), NCH, NE)
        al_id = view(carve(P), P)
        posm = view(carve(NCH * (NE * MAXPASS + 1)), NCH, NE * MAXPASS + 1)
        gatex = view(carve(NCH * (NE * MAXPASS + 1)), NCH, NE * MAXPASS + 1)
        small = view(carve(32), 32)
        b1 = view(carve(2 * F), 2 * F)
        hot = view(carve(NE * MAXPASS + 1), NE * MAXPASS + 1)
        sel = view(carve(NCH * SLOTS), NCH, SLOTS)
        esel = view(carve(SLOTS), SLOTS)
        gsel = view(carve(NCH * P), NCH, P)
        xsr = view(carve(512), 512)
        xs = view(carve(512), 4, P)
        gT = view(carve(S), S)
        hr = view(carve(512), 512)
        ur = view(carve(512), 512)
        sg = view(carve(512), 512)
        hT = view(carve(512), 4, P)
        ysb = view(carve(512), 512)
        bns = view(carve(2 * NCH * 6), NCH, 2, 6)
        mvar = view(carve(4), NCH, 2)
        assert top[0] <= POOLN
        w1s = [rview(q, 0, 2, 2 * F) for q in range(4)]
        w2s = [rview(4 + h, 0, 4, D) for h in range(2)]
        assert top[0] + SLOT <= POOLN
        w1x = [view(o, 2, 2 * F) for o in (top[0], o_s, o_xT)]

        ident = cst[:, C_ID:C_ID + P]
        bones = cst[:, C_BONE:C_BONE + P]
        ones = cst[:, C_ONES:C_ONES + P]
        hsel = cst[:, C_HSEL:C_HSEL + 2]

        def mask2(d):
            return cst[:, C_MASK2 + 256 * d:C_MASK2 + 256 * d + 256]

        def tri(d, inclusive):
            o = C_MASK2 + 256 * d + P * inclusive
            return cst[:, o:o + P]

        def gmask(d, n):
            o = C_GM + (d * len(LEVELS) + n) * P
            return cst[:, o:o + P]

        def par(name, i):
            return pcol[:, ROWS[name] + i:ROWS[name] + i + 1]

        LNO = {"gg": (0, GW), "gb": (GW, GW), "rg": (2 * GW, RW), "rb": (2 * GW + RW, RW),
               "mg": (2 * GW + 2 * RW, RW)}

        s_x = sem("x_loaded")
        s_par = sem("params_loaded")
        s_cst = sem("constants_loaded")
        s_small = sem("small_weights_loaded")
        s_lnb = sem("norm_rows_loaded")
        s_piece = {p: sem(f"w_in_{p}_loaded") for p in PIECES}
        s_wout = sem("w_out_loaded")
        s_late = sem("moe_small_loaded")
        s_ptr = sem("params_transposed")
        s_pev = sem("params_evacuated")
        s_xtr = sem("x_transposed")
        s_xev = sem("xT_evacuated")
        s_proj = sem("proj_tile_done")
        s_base = sem("proj_tile_read_by_act")
        s_shift = sem("proj_tile_shifted")
        s_lora = sem("lora_inputs_ready")
        s_z = sem("z_done")
        s_sig = sem("z_sigmoid_done")
        s_vtr = sem("v_transposed")
        s_vev = sem("vtok_evacuated")
        s_sq = sem("k_squares_ready")
        s_ss = sem("k_square_sums_done")
        s_kkd = sem("kk_ready")
        s_silu = sem("silu_sigmoid_done")
        s_rel = sem("decay_exponents_ready")
        s_exp = sem("decay_exps_done")
        s_ops = sem("scan_operands_ready")
        s_bon = sem("bonus_products_ready")
        s_prod = sem("products_done")
        s_prev = sem("products_evacuated")
        s_gps = sem("x2T_ready")
        s_x2 = sem("x2_transposed")
        s_xup = sem("x_evacuated")
        s_a = sem("level_product_done")
        s_g = sem("level_product_masked")
        s_xn = sem("level_update_done")
        s_bk = sem("bk_transposed")
        s_bkev = sem("bk_evacuated")
        s_w = sem("w_done")
        s_wev = sem("w_evacuated")
        s_u = sem("u_done")
        s_uev = sem("u_evacuated")
        s_h = sem("state_done")
        s_hev = sem("state_evacuated")
        s_o = sem("scan_out_done")
        s_oTe = sem("scan_outT_evacuated")
        s_ot = sem("scan_out_turned")
        s_oev = sem("scan_out_evacuated")
        s_gtr = sem("gate_rows_transposed")
        s_gact = sem("gate_exps_done")
        s_grow = sem("gate_rows_ready")
        s_gcol = sem("gate_cols_read")
        s_gcev = sem("stabilisers_ready")
        s_sc = sem("scores_done")
        s_mb = sem("m_rows_broadcast")
        s_arg = sem("decay_args_ready")
        s_de = sem("decay_factors_done")
        s_dm = sem("decay_factors_masked")
        s_pt = sem("weighted_scores_ready")
        s_pv = sem("num_den_done")
        s_hn = sem("mlstm_head_ready")
        s_gv = sem("gmlp_v_ready")
        s_gmix = sem("gmlp_mixed")
        s_bs = sem("gate_cols_and_bonus_sums_done")
        s_grp = sem("groups_ready")
        s_gT = sem("groups_transposed")
        s_gTe = sem("groupsT_evacuated")
        s_mix = sem("out_proj_done")
        s_x1 = sem("x1_ready")
        s_x1t = sem("x1_transposed")
        s_x1e = sem("x1T_evacuated")
        s_lg = sem("logits_done")
        s_rexp_in = sem("router_exp_ready")
        s_rexp = sem("router_exp_done")
        s_msk = sem("expert_mask_ready")
        s_pos = sem("positions_done")
        s_moe = sem("routing_ready")
        s_slot = [sem(f"slot{q}_loaded") for q in range(6)]
        s_slotx = [sem(f"odd_slot{q}_loaded") for q in range(3)]
        s_sel = sem("selection_ready")
        s_gath = sem("tokens_gathered")
        s_xs = sem("tokens_evacuated")
        s_gts = sem("gate_selection_transposed")
        s_gtev = sem("gate_selection_evacuated")
        s_w1 = sem("w1_piece_used")
        s_hg = sem("gate_half_ready")
        s_hs = sem("gate_sigmoid_done")
        s_ht = sem("hidden_ready")
        s_w2 = sem("w2_piece_used")
        s_yev = sem("expert_out_evacuated")
        s_xsr = sem("token_rows_evacuated")
        s_all = sem("all_experts_combined")
        s_out = sem("out_stored")
        s_fin = sem("x2_ready")
        s_gsel = sem("gate_selection_ready")
        s_zero = sem("zeros_ready")
        s_one = sem("ones_ready")
        s_qk = sem("qk_ready")
        s_gtr2 = sem("tokens_transposed")
        s_htr = sem("hidden_transposed")
        s_htev = sem("hiddenT_evacuated")
        s_hu = sem("up_half_clipped")
        s_hm = sem("gate_half_done")
        s_var = sem("variances_ready")
        s_std = sem("deviations_ready")
        s_kmx = sem("k_square_sums_read")
        s_msk_c = sem("masks_loaded")
        s_bias = sem("expert_biases_loaded")
        s_late2 = sem("ln2_loaded")
        s_bev = sem("bonus_sums_read")
        s_ksc = sem("key_scales_ready")
        s_kk2 = sem("unit_keys_ready")
        s_var2 = sem("row_variances_ready")
        s_std2 = sem("row_deviations_ready")
        s_al = sem("scaled_identity_ready")
        s_esel = sem("expert_row_selector_ready")
        s_esu = sem("expert_row_selector_used")
        s_dch = sem("dve_step")
        s_ach = sem("act_step")
        s_pch = sem("pool_step")

        w_in = t["w_in"][0].rearrange("(k p) n -> p k n", p=P)
        w_out = t["w_out"][0].rearrange("(k p) n -> p k n", p=P)
        ew1 = t["exp_w1"][0].rearrange("e (k p) n -> e p k n", p=P)
        ew2 = t["exp_w2"][0].rearrange("e (k p) n -> e p k n", p=P)
        x_d = t["x"][0].rearrange("(c p) d -> p c d", p=P)
        out_d = out[0].rearrange("(c p) d -> p c d", p=P)

        def row_bc(a):
            return a.unsqueeze(0).broadcast_to([P, a.shape[0]])

        block = ctx.enter_context(nc.Block())

        NPAR = 11

        @block.sync
        def _(sp):
            def load_piece(p):
                c0, n, slot = PIECES[p]
                sp.dma_start(rview(slot, 0, KD, n), w_in[:, :, c0:c0 + n]).then_inc(s_piece[p], 16)

            sp.dma_start(x_tok, x_d).then_inc(s_x, 16)
            load_piece("C")
            sp.wait_ge(s_par, 16 * NPAR)
            load_piece("A")
            sp.wait_ge(s_small, 16 * 4)
            for p in "BDE":
                load_piece(p)
            sp.dma_start(cst[:, C_MASK2:], t["consts"][:, C_MASK2:]).then_inc(s_msk_c, 16)
            load_piece("F")
            sp.wait_ge(s_proj, NT)
            load_piece("G")
            sp.wait_ge(s_proj, NT + 2)
            load_piece("H")
            sp.wait_ge(s_proj, NT + 4)
            sp.dma_start(wout[0], w_out[:, :, 0:512]).then_inc(s_wout, 16)
            sp.wait_ge(s_proj, NT + 6)
            sp.dma_start(wout[1], w_out[:, :, 512:1024]).then_inc(s_wout, 16)

            def load_slot(e, q, odd):
                if q < 4:
                    src = ew1[e][:, 2 * q:2 * q + 2]
                    if q < 3 and odd:
                        sp.dma_start(w1x[q], src).then_inc(s_slotx[q], 16)
                    else:
                        sp.dma_start(w1s[q], src).then_inc(s_slot[q], 16)
                else:
                    sp.dma_start(w2s[q - 4], ew2[e][:, 4 * (q - 4):4 * (q - 4) + 4]).then_inc(s_slot[q], 16)

            def first_parts(e, it, odd):
                for q in range(3):
                    sp.wait_ge(s_w1, it * 4 + (q - 7))
                    load_slot(e, q, odd)

            def last_parts(e, it):
                sp.wait_ge(s_w1, it * 4)
                load_slot(e, 3, False)
                for q in range(4, 6):
                    sp.wait_ge(s_w2, it * 2 + (q - 5))
                    load_slot(e, q, False)

            def from_second(it0):
                with sp.Fori(0, AHEAD // 2) as e2:
                    for odd in range(2):
                        e = e2 * 2 + odd
                        first_parts(e + 2, it0 + e + 2, odd)
                        last_parts(e + 1, it0 + e + 1)
                last_parts(AHEAD + 1, it0 + (AHEAD + 1))
                with sp.Fori(AHEAD // 2, NE // 2 - 1) as e2:
                    for odd in range(2):
                        e = e2 * 2 + odd
                        first_parts(e + 2, it0 + e + 2, odd)
                        last_parts(e + 2, it0 + e + 2)

            sp.wait_ge(s_ot, NP)
            for q in (2, 3, 5):
                load_slot(0, q, False)
            sp.wait_ge(s_grp, 7)
            for i, name in enumerate(("ln1_g", "ln1_b")):
                sp.dma_start(ln4[:, i], row_bc(t[name][0])).then_inc(s_late, 16)
            sp.dma_start(rw, t["router_w"][0].rearrange("(k p) e -> p k e", p=P)).then_inc(s_late, 16)
            sp.dma_start(rb, row_bc(t["router_b"][0])).then_inc(s_late, 16)
            sp.dma_start(b2[0:NE], t["exp_b2"][0]).then_inc(s_bias, 16)
            sp.dma_start(b1[0:NE], t["exp_b1"][0]).then_inc(s_bias, 16)
            load_slot(0, 4, False)
            load_slot(1, 0, True)
            sp.wait_ge(s_mix, 4)
            for q in (0, 1):
                load_slot(0, q, False)
            sp.wait_ge(s_x1, NCH)
            load_slot(1, 1, True)
            sp.wait_ge(s_lg, 1)
            load_slot(1, 2, True)
            from_second(0)
            sp.wait_ge(s_moe, 2)
            npass = sp.value_load(npass_i[0:1, 0:1], min_val=1, max_val=MAXPASS)
            with sp.If(npass > 1):
                with sp.Fori(1, npass) as p:
                    first_parts(0, p * NE, False)
                    last_parts(0, p * NE)
                    first_parts(1, p * NE + 1, True)
                    from_second(p * NE)
            sp.wait_ge(s_gts, npass * NE)
            for i, name in enumerate(("ln2_g", "ln2_b")):
                sp.dma_start(ln4[:, 2 + i], row_bc(t[name][0])).then_inc(s_late2, 16)
            for c in range(NCH):
                sp.wait_ge(s_fin, c + 1)
                sp.dma_start(out_d[:, c], x_tok[:, c]).then_inc(s_out, 16)
            sp.wait_ge(s_out, 16 * NCH)

        @block.scalar
        def _(act):
            A = nc.scalar.activation
            roots = [0]
            achain = [1]
            act.dma_start(cst[:, 0:C_MASK2], t["consts"][:, 0:C_MASK2]).then_inc(s_cst, 16)
            rows = [("mu0", t["rwkv_mu"][0, 0:1]), ("mu1", t["rwkv_mu"][0, 1:2]), ("w0", t["rwkv_w0"][0]),
                    ("a0", t["rwkv_a0"][0]), ("kk", t["rwkv_k_k"]), ("ka", t["rwkv_k_a"]),
                    ("rk", t["rwkv_r_k"].rearrange("l h d -> l (h d)")), ("cw", t["mlstm_conv_w"][0]),
                    ("cb", t["mlstm_conv_b"]), ("bs", t["gmlp_bs"][0])]
            for name, src in rows:
                n = src.shape[0] * src.shape[1] // P
                act.dma_start(prow[ROWS[name]:ROWS[name] + n, :],
                              src.rearrange("a (n p) -> (a n) p", p=P)).then_inc(s_par, 16)
            act.dma_start(wsraw, t["gmlp_ws"][0].rearrange("h p q -> p h q")).then_inc(s_par, 16)
            act.dma_start(lora2[0:64], t["rwkv_w2"][0].rearrange("d r c -> r d c")).then_inc(s_small, 16)
            act.dma_start(lora2[64:128], t["rwkv_a2"][0].rearrange("d r c -> r d c")).then_inc(s_small, 16)
            act.dma_start(g2, t["rwkv_g2"][0]).then_inc(s_small, 16)
            act.dma_start(gbias[0:6, :], t["mlstm_gate_b"][0].rearrange("(k h) -> h k", h=RH),
                          allow_slow_non_contiguous=True).then_inc(s_small, 16)
            for g in range(4):
                act.wait_ge(s_xtr, g + 1)
                A(xT[:, 2 * g:2 * g + 2, :], pview(g, 0, 2, S), ACT.Copy).then_inc(s_xev, 1)

            def base_of(i):
                act.wait_ge(s_proj, i + 1)
                if i >= 2:
                    act.wait_ge(s_shift, i - 1)
                piece, col, kind, j = T_TILES[i]
                if i < NR:
                    if i == 0:
                        act.wait_ge(s_pev, 2)
                    m = MU_COL[kind] + (j if kind in "rkv" else 0)
                    A(base[:, i % 2], bank[i % 4][:, 0:S], ACT.Copy, scale=own[:, m:m + 1]).then_inc(s_base, 1)
                else:
                    A(base[:, i % 2], bank[i % 4][:, 0:S], ACT.Identity, bias=par("cb", j),
                      scale=par("cw", 6 + j)).then_inc(s_base, 1)

            def z_sigmoids(pt):
                act.wait_ge(s_z, pt + 1)
                b = 4 + 2 * (pt % 2)
                for d in range(2):
                    A(sigw[:, pt, d], bank[b][:, S * d:S * d + S], ACT.Sigmoid, bias=par("w0", 3 * d + pt))
                    last = A(icl[:, pt, d], bank[b + 1][:, S * d:S * d + S], ACT.Sigmoid,
                             bias=par("a0", 3 * d + pt))
                last.then_inc(s_sig, 1)

            for i in range(NR):
                base_of(i)
                if i == 3:
                    act.wait_ge(s_shift, 2)
                    A(wa[0:64], wa[0:64], ACT.Tanh).then_inc(s_lora, 1)
                if i == 4:
                    act.wait_ge(s_shift, 3)
                    A(gd, gd, ACT.Sigmoid).then_inc(s_lora, 1)
            z_sigmoids(0)
            z_sigmoids(1)
            base_of(11)
            base_of(12)
            z_sigmoids(2)
            base_of(13)
            base_of(14)
            act.wait_ge(s_kmx, 2)
            A(kk, kk, ACT.Sqrt).then_inc(s_kkd, 1)
            act.wait_ge(s_vtr, 1)
            A(vtok[:, 0], bank[4][:, 0:RW], ACT.Copy)
            A(vtok[:, 1], bank[5][:, 0:RW], ACT.Copy).then_inc(s_vev, 1)
            base_of(15)
            base_of(16)
            act.wait_ge(s_vtr, 2)
            A(gate_r[:, 0], bank[6][:, 0:RW], ACT.Copy)
            A(gate_r[:, 1], bank[7][:, 0:RW], ACT.Copy).then_inc(s_vev, 1)
            act.wait_ge(s_shift, NT)
            A(sgq, qk, ACT.Sigmoid).then_inc(s_silu, 1)
            for j in range(4):
                piece, c = TOK_TILES[j]
                act.wait_ge(s_proj, NT + j + 1)
                b = bank[(NT + j) % 4]
                if piece == "F":
                    A(mv[:, c, :, 0:HD], b[:, 0:RW].rearrange("p (h e) -> p h e", h=RH), ACT.Copy).then_inc(s_base, 1)
                else:
                    A(osig[:, c], b[:, 0:RW], ACT.Sigmoid)
                    A(gt[:, c], b[:, RW:RW + 24], ACT.Copy).then_inc(s_base, 1)

            def inv_root(which):
                roots[0] += 1
                act.wait_ge(s_var, roots[0])
                v = stat[which][1]
                A(v, v, ACT.Ln).then_inc(s_ach, 1)
                achain[0] += 1
                act.wait_ge(s_ach, achain[0])
                A(v, v, ACT.Exp, scale=-0.5).then_inc(s_std, 1)

            def key_scales(pt):
                if pt:
                    act.wait_ge(s_bon, pt)
                A(rrk, rT[:, pt], ACT.Copy, scale=par("rk", pt))
                A(kka, kT[:, pt], ACT.Copy, scale=par("ka", pt)).then_inc(s_ksc, 1)

            def decay_exps(pt):
                act.wait_ge(s_rel, pt + 1)
                A(e_inv, srel, ACT.Exp, scale=KAPPA)
                A(e_inc, srel, ACT.Exp, scale=-KAPPA)
                A(gam[:, pt % 2], gam[:, pt % 2], ACT.Exp, scale=-KAPPA)
                A(s_exc, s_exc, ACT.Exp, scale=-KAPPA).then_inc(s_exp, 1)

            act.wait_ge(s_kk2, 1)
            key_scales(0)
            decay_exps(0)
            for j in (4, 5):
                act.wait_ge(s_proj, NT + j + 1)
                A(gel[:, j - 4], bank[(NT + j) % 4][:, 0:512], ACT.Gelu).then_inc(s_base, 1)
            act.wait_ge(s_grow, 1)
            A(row1[0:6], row1[0:6], ACT.Exp, scale=-1.0).then_inc(s_ach, 1)
            act.wait_ge(s_ach, 1)
            A(row1[0:6], row1[0:6], ACT.Ln, bias=1.0).then_inc(s_gact, 1)

            def factors(h):
                act.wait_ge(s_arg, h + 1)
                A(ebuf, ebuf, ACT.Exp, scale=-1.0).then_inc(s_de, 1)

            for pt in range(NP):
                for d in range(2):
                    act.wait_ge(s_bk, 2 * pt + d + 1)
                    for h in range(2):
                        hc = slice(HD * h, HD * h + HD)
                        last = A(bktok[:, d, :, hc], pview(4 * d + 2, 0, 2, 2, P)[:, :, h, hc], ACT.Copy)
                    last.then_inc(s_bkev, 1)
                for d in range(2):
                    act.wait_ge(s_x2, 2 * pt + d + 1)
                    A(xm[:, d], pview(1 + 4 * d, 0, 4, P), ACT.Copy).then_inc(s_xup, 1)
                for n in range(len(LEVELS)):
                    for d in range(2):
                        act.wait_ge(s_xn, 12 * pt + 2 * n + d + 1)
                        if n < len(LEVELS) - 1:
                            A(xm[:, d], pview(1 + 4 * d, 0, 4, P), ACT.Copy)
                        A(xmT[:, d], pview(2 + 4 * d, 0, 4, P), ACT.Copy).then_inc(s_xup, 1)
                    if n == 0 and pt:
                        inv_root("r")
                    if n == 1:
                        if pt == 0:
                            act.wait_ge(s_gcol, 1)
                            A(emt, emt, ACT.Exp, scale=-1.0).then_inc(s_gcev, 1)
                        factors(2 * pt)
                        if pt + 1 < NP:
                            key_scales(pt + 1)
                    if n == 2:
                        inv_root("m" if pt else "g")
                    if n == 3:
                        if pt + 1 < NP:
                            decay_exps(pt + 1)
                        factors(2 * pt + 1)
                for step in range(2):
                    for d in range(2):
                        c = d if step == 0 else 1 - d
                        act.wait_ge(s_w, 4 * pt + 2 * step + d + 1)
                        A(wbuf[:, d, c::2], pview(4 * d + 1, 0, 2, HD), ACT.Copy).then_inc(s_wev, 1)
                    for d in range(2):
                        c = d if step == 0 else 1 - d
                        act.wait_ge(s_u, 4 * pt + 2 * step + d + 1)
                        A(ubuf[:, d, c::2], pview(4 * d + 2, 256, 4, HD)[:, c::2], ACT.Copy).then_inc(s_uev, 1)
                    if step == 0:
                        for d in range(2):
                            act.wait_ge(s_h, 2 * pt + d + 1)
                            for h in range(2):
                                hp = slice(HD * h, HD * h + HD)
                                last = A(hst[hp, d, hp], bank[4 * d][hp, 0:HD], ACT.Copy, scale=gam[hp, pt % 2, d:d + 1])
                            last.then_inc(s_hev, 1)
                        if pt == NP - 1:
                            inv_root("m")
                act.wait_ge(s_o, pt + 1)
                A(oT, pview(3, 0, NCH, P), ACT.Copy).then_inc(s_oTe, 1)
            for g in range(3):
                act.wait_ge(s_gT, g + 1)
                A(xT[:, 2 * g:2 * g + 2, :], pview(g, 0, 2, S), ACT.Copy).then_inc(s_gTe, 1)
            inv_root("r")
            act.wait_ge(s_gT, 4)
            A(xT[:, 6:8, :], pview(3, 0, 2, S), ACT.Copy).then_inc(s_gTe, 1)
            def wide_root(n):
                act.wait_ge(s_var2, n)
                v = mvar[:, (n - 1) % 2, 1:2]
                achain[0] += 1
                A(v, v, ACT.Ln).then_inc(s_ach, 1)
                act.wait_ge(s_ach, achain[0])
                A(v, v, ACT.Exp, scale=-0.5).then_inc(s_std2, 1)

            for c in range(NCH):
                wide_root(c + 1)
                for q in range(2):
                    act.wait_ge(s_x1t, 2 * c + q + 1)
                    A(xT[:, 4 * q:4 * q + 4, P * c:P * c + P], pview(2 * c + q, 0, 4, P), ACT.Copy).then_inc(s_x1e, 1)
            act.wait_ge(s_rexp_in, 1)
            for c in range(NCH):
                last = A(gates[:, c], lg[:, c], ACT.Exp, bias=small[:, c:c + 1])
            last.then_inc(s_rexp, 1)

            act.wait_ge(s_gath, 1)
            A(xsr, bank[7][:, :], ACT.Copy).then_inc(s_xsr, 1)
            act.wait_ge(s_gtr2, 1)
            A(xs, pview(7, 0, 4, P), ACT.Copy).then_inc(s_xs, 1)
            act.wait_ge(s_moe, 2)
            npass = act.value_load(npass_i[0:1, 0:1], min_val=1, max_val=MAXPASS)
            with act.Fori(0, npass) as p:
                with act.Fori(0, NE) as e:
                    it = p * NE + e
                    act.wait_ge(s_gts, it + 1)
                    A(gT, bank[6][:, 0:S], ACT.Copy).then_inc(s_gtev, 1)
                    act.wait_ge(s_hg, it + 1)
                    A(sg, hr, ACT.Sigmoid, scale=1.702).then_inc(s_hs, 1)
                    act.wait_ge(s_gath, it + 2)
                    A(xsr, bank[7][:, :], ACT.Copy).then_inc(s_xsr, 1)
                    act.wait_ge(s_htr, it + 1)
                    A(hT, pview(4, 0, 4, P), ACT.Copy).then_inc(s_htev, 1)
                    act.wait_ge(s_gtr2, it + 2)
                    A(xs, pview(7, 0, 4, P), ACT.Copy).then_inc(s_xs, 1)
                    act.wait_ge(s_w2, it * 2 + 2)
                    A(ysb, bank[6][:, :], ACT.Copy).then_inc(s_yev, 1)
            wide_root(3)
            wide_root(4)

        @block.tensor
        def _(pe):
            mm = nc.tensor.matmul
            tr = nc.tensor.transpose
            pe.wait_ge(s_cst, 16)
            pe.wait_ge(s_x, 16)
            for g in range(4):
                for k in range(2):
                    for c in range(NCH):
                        last = tr(pview(g, 0, 2, S)[:, k, P * c:P * c + P],
                                  x_tok[:, c, P * (2 * g + k):P * (2 * g + k + 1)], ident)
                last.then_inc(s_xtr, 1)
            pe.wait_ge(s_par, 16 * NPAR)
            tr(bank[4][:, 0:NROWS], prow[0:NROWS, :], ident[0:NROWS, 0:NROWS])
            for g in range(4):
                last = tr(bank[5][:, P * g:P * g + P], wsraw[:, g], ident)
            last.then_inc(s_ptr, 1)
            pe.wait_ge(s_xev, 4)

            loaded = []

            def piece_ready(p):
                if p not in loaded:
                    pe.wait_ge(s_piece[p], 16)
                    loaded.append(p)

            def bank_free(i):
                if i >= 4:
                    if i - 4 < NT:
                        pe.wait_ge(s_shift, i - 3)
                    else:
                        pe.wait_ge(s_base, i - 3)

            def t_tile(i):
                p, col, _, _ = T_TILES[i]
                piece_ready(p)
                bank_free(i)
                w = rview(PIECES[p][2], 0, KD, PIECES[p][1])
                for k in range(KD):
                    last = mm(bank[i % 4][:, 0:S], w[:, k, col:col + P], xT[:, k], start=(k == 0), stop=(k == KD - 1))
                last.then_inc(s_proj, 1)

            def tok_tile(j):
                p, c = TOK_TILES[j]
                piece_ready(p)
                bank_free(NT + j)
                n = PIECES[p][1]
                w = rview(PIECES[p][2], 0, KD, n)
                for k in range(KD):
                    last = mm(bank[(NT + j) % 4][:, 0:n], xT[:, k, P * c:P * c + P], w[:, k, :],
                              start=(k == 0), stop=(k == KD - 1))
                last.then_inc(s_proj, 1)

            def z_tiles(pt):
                b = 4 + 2 * (pt % 2)
                if pt == 2:
                    pe.wait_ge(s_sig, 1)
                for d in range(2):
                    mm(bank[b][:, S * d:S * d + S], lora2[0:64, d, P * pt:P * pt + P], wa[0:64], start=True, stop=True)
                for d in range(2):
                    last = mm(bank[b + 1][:, S * d:S * d + S], lora2[64:128, d, P * pt:P * pt + P], wa[64:128],
                              start=True, stop=True)
                last.then_inc(s_z, 1)

            for i in range(NR):
                t_tile(i)
            pe.wait_ge(s_lora, 1)
            pe.wait_ge(s_small, 64)
            pe.wait_ge(s_pev, 1)
            z_tiles(0)
            z_tiles(1)
            t_tile(11)
            t_tile(12)
            z_tiles(2)
            pe.wait_ge(s_sig, 2)
            pe.wait_ge(s_sq, 1)
            kf = kksq.rearrange("p a s -> p (a s)")
            mm(bank[6][:, 0:512], bones, kf[:, 0:512], start=True, stop=True)
            mm(bank[7][:, 0:S], bones, kf[:, 512:768], start=True, stop=True).then_inc(s_ss, 1)
            t_tile(13)
            t_tile(14)
            pe.wait_ge(s_sig, 3)
            for c in range(NCH):
                for pt in range(NP):
                    last = tr(bank[4 + c][:, P * pt:P * pt + P], vT[:, pt, P * c:P * c + P], ident)
            last.then_inc(s_vtr, 1)
            t_tile(15)
            t_tile(16)
            pe.wait_ge(s_kmx, 2)
            pe.wait_ge(s_lora, 2)
            for c in range(NCH):
                last = mm(bank[6 + c][:, 0:RW], gd[:, P * c:P * c + P], g2, start=True, stop=True)
            last.then_inc(s_vtr, 1)
            for j in range(6):
                tok_tile(j)
            pe.wait_ge(s_base, NT + 4)
            pe.wait_ge(s_vev, 1)
            for k in range(4):
                for c in range(NCH):
                    last = tr(bank[4 + k // 2][0:RH, S * (k % 2) + P * c:S * (k % 2) + P * c + P],
                              gt[:, c, RH * k:RH * k + RH], ident)
            last.then_inc(s_gtr, 1)

            def m_rows(h):
                if h:
                    pe.wait_ge(s_pt, h)
                for d in range(2):
                    last = mm(bank[3][:, S * d:S * d + S], cst[0:RH, C_SELM + P * h:C_SELM + P * h + P],
                              row1[0:RH, d], start=True, stop=True)
                last.then_inc(s_mb, 1)

            def scores(h):
                pe.wait_ge(s_arg, h + 1)
                hp = slice(HD * (h % 2), HD * (h % 2) + HD)
                for sc in range(NCH):
                    last = mm(bank[3][:, S * sc:S * sc + S], qk[hp, 3 + h // 2, P * sc:P * sc + P], qk[hp, h // 2],
                              start=True, stop=True)
                last.then_inc(s_sc, 1)

            def weigh(h):
                pe.wait_ge(s_pt, h + 1)
                pe.wait_ge(s_bev, h // 2 + 1)
                if h:
                    pe.wait_ge(s_hn, h)
                nd = pview(7, 0, 2, NCH, 65)
                for d, c, parts in ((0, 0, ((0, 0),)), (0, 1, ((0, P), (1, S))),
                                    (1, 0, ((0, 0), (1, P))), (1, 1, ((1, S),))):
                    for n, (sc, col) in enumerate(parts):
                        last = mm(nd[:, d, c], pbuf[:, d, col:col + P], mv[:, sc, h], start=(n == 0),
                                  stop=(n == len(parts) - 1))
                last.then_inc(s_pv, 1)

            def gate_cols():
                pe.wait_ge(s_grow, 2)
                for kind, r in ((0, row3), (1, row0)):
                    for d in range(2):
                        for c in range(NCH):
                            i = 12 * (2 * kind + d) + RH * c
                            tr(bank[7][:, i:i + RH], r[0:RH, d, P * c:P * c + P], ident[0:RH, 0:RH])

            def scans_turned(pt):
                pe.wait_ge(s_oTe, pt + 1)
                pe.wait_ge(s_hn, 2 * pt + 2)
                for c in range(NCH):
                    last = tr(bank[7][:, P * c:P * c + P], oT[:, c], ident)
                last.then_inc(s_ot, 1)

            def bonus_sums(pt):
                if pt:
                    pe.wait_ge(s_oev, pt)
                pe.wait_ge(s_bon, pt + 1)
                for c in range(NCH):
                    last = mm(bank[7][:, 64 + 2 * c:66 + 2 * c], bon[:, pt, P * c:P * c + P], hsel, start=True, stop=True)
                last.then_inc(s_bs, 1)

            pe.wait_ge(s_base, NT + 6)
            pe.wait_ge(s_vev, 2)
            pe.wait_ge(s_grow, 1)
            pe.wait_ge(s_qk, 1)
            pe.wait_ge(s_one, 1)
            pe.wait_ge(s_msk_c, 16)
            for pt in range(NP):
                ar = ar_[pt % 2]
                pe.wait_ge(s_ops, pt + 1)
                for n, (d, f, b) in enumerate(FILLS):
                    h = f % 2
                    if f == 1:
                        pe.wait_ge(s_prev, 8 * pt + 1 + 2 * d)
                    for c in range(NCH):
                        last = mm(pview(4 * d + b, 0, 2, 256)[:, c], (ktz, btz)[f // 2][h][:, d, c],
                                  ar[:, d, c].rearrange("p a t -> p (a t)"), start=True, stop=True)
                    last.then_inc(s_prod, 1)
                    if n == 3 and pt:
                        scans_turned(pt - 1)
                for d in range(2):
                    pe.wait_ge(s_prev, 8 * pt + 5 + 2 * d)
                    for h in range(2):
                        tr(pview(4 * d + 2, 0, 2, 2, P)[:, 0, h], btz[h][:, d, d], ident)
                        last = tr(pview(4 * d + 2, 0, 2, 2, P)[:, 1, h], ktz[h][:, d, d], ident)
                    last.then_inc(s_bk, 1)
                for d in range(2):
                    pe.wait_ge(s_gps, 2 * pt + d + 1)
                    for j in range(4):
                        last = tr(pview(1 + 4 * d, 0, 4, P)[:, j], xmT[:, d, j], ident)
                    last.then_inc(s_x2, 1)
                for n in range(len(LEVELS)):
                    for d in range(2):
                        pe.wait_ge(s_xup, 14 * pt + 2 * n + d + 1)
                        if n == 0:
                            pe.wait_ge(s_prev, 8 * pt + 6 + 2 * d)
                        for j in range(4):
                            last = mm(pview(4 * d, 0, 4, P)[:, j], mpT[:, d, j, 0:P], xm[:, d, j], start=True, stop=True)
                        last.then_inc(s_a, 1)
                    if n == 1:
                        if pt == 0:
                            gate_cols()
                        bonus_sums(pt)
                        m_rows(2 * pt)
                    for d in range(2):
                        pe.wait_ge(s_g, 12 * pt + 2 * n + d + 1)
                        if n == 0:
                            pe.wait_ge(s_bkev, 2 * pt + d + 1)
                        for j in range(4):
                            if n < len(LEVELS) - 1:
                                mm(pview(1 + 4 * d, 0, 4, P)[:, j], xmT[:, d, j], gm[:, d, j], start=True, stop=True)
                            last = mm(pview(2 + 4 * d, 0, 4, P)[:, j], gm[:, d, j], xmT[:, d, j], start=True, stop=True)
                        last.then_inc(s_xn, 1)
                    if n == 1:
                        scores(2 * pt)
                    if n == 2:
                        weigh(2 * pt)
                        m_rows(2 * pt + 1)
                    if n == 3:
                        scores(2 * pt + 1)
                    if n == 4:
                        weigh(2 * pt + 1)
                    if n == 5 and pt == NP - 1:
                        pe.wait_ge(s_gv, 1)
                        for g in range(4):
                            last = mm(pview(3, P * g, NCH, HD), wsT[:, g], gel[:, :, GW + HD * g:GW + HD * g + HD],
                                      start=True, stop=True)
                        last.then_inc(s_gmix, 1)

                def v_of(c, h):
                    return vtok[:, c, HD * (2 * pt + h):HD * (2 * pt + h) + HD]

                for step in range(2):
                    for d in range(2):
                        c = d if step == 0 else 1 - d
                        if step == 1:
                            pe.wait_ge(s_hev, 2 * pt + d + 1)
                        w = bank[4 * d + 1]
                        if step == 1:
                            mm(w[:, 0:P], ar[:, d, c, 0], hst[:, d], start=True, stop=False)
                        for h in range(2):
                            last = mm(w[:, HD * h:HD * h + HD], nqT[:, d, 2 * h + c, 0:P], v_of(c, h), start=(step == 0),
                                      stop=(step == 0 or h == 1))
                        last.then_inc(s_w, 1)
                    for d in range(2):
                        c = d if step == 0 else 1 - d
                        pe.wait_ge(s_wev, 4 * pt + 2 * step + d + 1)
                        if step == 0:
                            pe.wait_ge(s_xup, 14 * pt + 12 + d + 1)
                        for h in range(2):
                            j = 2 * h + c
                            last = mm(pview(4 * d + 2, 256, 4, HD)[:, j], xmT[:, d, j], wbuf[:, d, j], start=True, stop=True)
                        last.then_inc(s_u, 1)
                    if step == 0:
                        for d in range(2):
                            pe.wait_ge(s_uev, 4 * pt + d + 1)
                            for h in range(2):
                                hp = slice(HD * h, HD * h + HD)
                                mm(bank[4 * d][hp, 0:HD], bktok[:, d, 0, hp], ubuf[:, d, 2 * h + d], start=True, stop=False)
                                last = mm(bank[4 * d][hp, 0:HD], bktok[:, d, 1, hp], v_of(d, h), start=False, stop=True)
                            last.then_inc(s_h, 1)
                pe.wait_ge(s_uev, 4 * pt + 4)
                if pt == NP - 1:
                    pe.wait_ge(s_grp, 5)
                for c in range(NCH):
                    for d in range(2):
                        for h in range(2):
                            j = 2 * h + c
                            mm(bank[3][HD * h:HD * h + HD, P * c:P * c + P], ubuf[:, d, j], mpT[:, d, j, P:2 * P],
                               start=(d == 0), stop=False)
                        for h in range(2):
                            j = 2 * h + c
                            mm(bank[3][HD * h:HD * h + HD, P * c:P * c + P], v_of(c, h), nqT[:, d, j, P:2 * P],
                               start=False, stop=False)
                    last = mm(bank[3][:, P * c:P * c + P], hst[:, 1 - c], ar[:, 1 - c, c, 1], start=False, stop=True)
                last.then_inc(s_o, 1)

            pe.wait_ge(s_wout, 32)
            for g, (ka, kb) in enumerate(OUT_ORDER):
                pe.wait_ge(s_grp, 7 if g == 3 else 6)
                for n, k in enumerate((ka, kb)):
                    for c in range(NCH):
                        last = tr(pview(g, 0, 2, S)[:, n, P * c:P * c + P], grp[:, c, P * k:P * k + P], ident)
                last.then_inc(s_gT, 1)
                if g == 2:
                    scans_turned(NP - 1)
                    pe.wait_ge(s_gTe, 3)
                    for c in range(NCH):
                        if c == 1:
                            pe.wait_ge(s_oev, NP)
                        for hf in range(2):
                            for k in range(6):
                                mm(bank[4 + 2 * c + hf][:, :], xT[:, k, P * c:P * c + P],
                                   wout[hf][:, OUT_ORDER[k // 2][k % 2]], start=(k == 0), stop=False)
            pe.wait_ge(s_gTe, 4)
            for c in range(NCH):
                for hf in range(2):
                    for k in (6, 7):
                        last = mm(bank[4 + 2 * c + hf][:, :], xT[:, k, P * c:P * c + P],
                                  wout[hf][:, OUT_ORDER[k // 2][k % 2]], start=False, stop=(k == 7))
                    last.then_inc(s_mix, 1)
            pe.wait_ge(s_late, 16 * 4)
            for c in range(NCH):
                pe.wait_ge(s_x1, c + 1)
                for q in range(2):
                    for k in range(4):
                        last = tr(pview(2 * c + q, 0, 4, P)[:, k], x_tok[:, c, P * (4 * q + k):P * (4 * q + k + 1)], ident)
                    last.then_inc(s_x1t, 1)
                for k in range(KD):
                    if k % 4 == 0:
                        pe.wait_ge(s_x1e, 2 * c + k // 4 + 1)
                    last = mm(bank[4][:, NE * c:NE * c + NE], xT[:, k, P * c:P * c + P], rw[:, k], start=(k == 0), stop=(k == KD - 1))
            last.then_inc(s_lg, 1)
            pe.wait_ge(s_al, 1)
            for c in range(NCH):
                for hf in range(2):
                    mm(bank[2 * c + hf][:, :], al_id, x_tok[:, c, 512 * hf:512 * hf + 512], start=True, stop=False,
                       skip_group_check=True)
            pe.wait_ge(s_msk, 1)
            mm(bank[5][:, 0:NE], tri(0, 0), msk[:, 0], start=True, stop=True)
            mm(bank[5][:, NE:2 * NE], ones, msk[:, 0], start=True, stop=False)
            mm(bank[5][:, NE:2 * NE], tri(0, 0), msk[:, 1], start=False, stop=True)
            mm(bank[5][:, 2 * NE:3 * NE], ones, msk[:, 0], start=True, stop=False)
            mm(bank[5][:, 2 * NE:3 * NE], ones, msk[:, 1], start=False, stop=True).then_inc(s_pos, 1)
            def gather_rows():
                for c in range(NCH):
                    for hf in range(2):
                        last = mm(bank[7][SLOTS * hf:SLOTS * hf + SLOTS, :], sel[:, c], x_tok[:, c, 512 * hf:512 * hf + 512],
                                  start=(c == 0), stop=(c == NCH - 1))
                last.then_inc(s_gath, 1)

            def gather_turn(n):
                pe.wait_ge(s_xsr, n)
                for j in range(4):
                    last = tr(pview(7, 0, 4, P)[:, j], xsr[:, P * j:P * j + P], ident)
                last.then_inc(s_gtr2, 1)

            def combine(c, stop):
                for hf in range(2):
                    hp = slice(SLOTS * hf, SLOTS * hf + SLOTS)
                    last = mm(bank[2 * c + hf][:, :], gT[hp, P * c:P * c + P], ysb[hp, :], start=False, stop=stop,
                              skip_group_check=True)
                return last

            def expert(it, turn, odd):
                pe.wait_ge(s_esel, it + 1)
                for g in range(2):
                    for hf in range(2):
                        hp = slice(SLOTS * hf, SLOTS * hf + SLOTS)
                        mm(bank[4 + g][hp, :], esel[0:NE], b1[0:NE, F * g + 512 * hf:F * g + 512 * hf + 512],
                           start=True, stop=False)
                pe.wait_ge(s_xs, it + 1)
                for q in range(4):
                    if q < 3:
                        pe.wait_ge((s_slotx if odd else s_slot)[q], turn * 16 + 16)
                    else:
                        pe.wait_ge(s_slot[q], it * 16 + 16)
                    w = w1x[q] if odd and q < 3 else w1s[q]
                    for k in (2 * q, 2 * q + 1):
                        lhs = xs[:, k % 4, SLOTS * (k // 4):SLOTS * (k // 4) + SLOTS]
                        for g in range(2):
                            for hf in range(2):
                                hp = slice(SLOTS * hf, SLOTS * hf + SLOTS)
                                o = F * g + 512 * hf
                                last = mm(bank[4 + g][hp, :], lhs, w[:, k % 2, o:o + 512], start=False,
                                          stop=(k == KD - 1))
                    last.then_inc(s_w1, 1)
                    if q == 0:
                        pe.wait_ge(s_yev, it + 1)
                        for c in range(NCH):
                            combine(c, False)
                    if q == 1:
                        pe.wait_ge(s_gsel, it + 1)
                        for c in range(NCH):
                            last = tr(bank[6][:, P * c:P * c + P], gsel[:, c], ident)
                        last.then_inc(s_gts, 1)
                pe.wait_ge(s_sel, it + 2)
                gather_rows()
                pe.wait_ge(s_gtev, it + 1)
                for hf in range(2):
                    last = mm(bank[6][SLOTS * hf:SLOTS * hf + SLOTS, :], esel[0:NE], b2[0:NE, 512 * hf:512 * hf + 512],
                              start=True, stop=False)
                last.then_inc(s_esu, 1)
                pe.wait_ge(s_ht, it + 1)
                for j in range(4):
                    last = tr(pview(4, 0, 4, P)[:, j], hr[:, P * j:P * j + P], ident)
                last.then_inc(s_htr, 1)
                gather_turn(it + 2)
                pe.wait_ge(s_htev, it + 1)
                for k in range(KD):
                    if k % 4 == 0:
                        pe.wait_ge(s_slot[4 + k // 4], it * 16 + 16)
                    for hf in range(2):
                        last = mm(bank[6][SLOTS * hf:SLOTS * hf + SLOTS, :],
                                  hT[:, k % 4, SLOTS * (k // 4):SLOTS * (k // 4) + SLOTS],
                                  w2s[k // 4][:, k % 4, 512 * hf:512 * hf + 512], start=False, stop=(k == KD - 1))
                    if k % 4 == 3:
                        last.then_inc(s_w2, 1)

            pe.wait_ge(s_sel, 1)
            gather_rows()
            gather_turn(1)
            pe.wait_ge(s_bias, 32)
            pe.wait_ge(s_zero, 1)
            pe.wait_ge(s_moe, 2)
            npass = pe.value_load(npass_i[0:1, 0:1], min_val=1, max_val=MAXPASS)
            with pe.Fori(0, npass) as p:
                with pe.Fori(0, NE // 2) as e2:
                    for odd in range(2):
                        expert(p * NE + e2 * 2 + odd, p * (NE // 2) + e2, odd)
            pe.wait_ge(s_yev, npass * NE + 1)
            for c in range(NCH):
                combine(c, True).then_inc(s_all, 1)

        @block.gpsimd
        def _(pool):
            nc.gpsimd.memset(hst, 0.0)
            nc.gpsimd.memset(mv[:, :, :, HD:HD + 1], 1.0).then_inc(s_one, 1)
            pool.wait_ge(s_piece["B"], 16)
            for k, src in (("gg", "gmlp_ln_g"), ("gb", "gmlp_ln_b"), ("rg", "rwkv_ln_g"), ("rb", "rwkv_ln_b"),
                           ("mg", "mlstm_ln_g")):
                o, n = LNO[k]
                pool.dma_start(lnb[:, o:o + n], row_bc(t[src][0])).then_inc(s_lnb, 16)
            def mask_factors(h):
                pool.wait_ge(s_de, h + 1)
                for d in range(2):
                    diag = ebuf[:, d].rearrange("p (b t) -> p b t", b=3)[:, 0::2]
                    last = nc.gpsimd.tensor_tensor(diag, diag, tri(d, 1).unsqueeze(1).broadcast_to([P, 2, P]), ALU.mult)
                last.then_inc(s_dm, 1)

            for pt in range(NP):
                for d in range(2):
                    pool.wait_ge(s_prev, 8 * pt + 2 + 2 * d)
                    m = mpT[:, d, :, 0:P]
                    nc.gpsimd.tensor_tensor(m, m, ident.unsqueeze(1).broadcast_to([P, 4, P]), ALU.add).then_inc(s_pch, 1)
                    pool.wait_ge(s_pch, 2 * pt + d + 1)
                    x2 = cst[:, C_X2 + P * d:C_X2 + P * d + P]
                    nc.gpsimd.tensor_tensor(xmT[:, d], m, x2.unsqueeze(1).broadcast_to([P, 4, P]), ALU.mult).then_inc(s_gps, 1)
                mask_factors(2 * pt)
                mask_factors(2 * pt + 1)
            pool.wait_ge(s_grp, 7)
            nc.gpsimd.memset(gT, 0.0).then_inc(s_zero, 1)
            nc.gpsimd.memset(ysb, 0.0).then_inc(s_yev, 1)

        @block.vector
        def _(dve):
            steps = [0]
            norms = [0]
            V = nc.vector

            def link(ins):
                steps[0] += 1
                ins.then_inc(s_dch, 1)
                dve.wait_ge(s_dch, steps[0])

            def norm_a(which, a, tmp, w, eps):
                g = a.shape[1]
                mean, var = stat[which][0][:, 0:g], stat[which][1][:, 0:g]
                link(V.tensor_reduce(mean, a, X, ALU.add))
                link(V.tensor_scalar(mean, mean, 1.0 / w, None, ALU.mult))
                link(V.tensor_tensor(a, a, spread(mean, w), ALU.subtract))
                link(V.tensor_tensor(tmp, a, a, ALU.mult))
                link(V.tensor_reduce(var, tmp, X, ALU.add))
                V.tensor_scalar(var, var, 1.0 / w, eps, ALU.mult, ALU.add).then_inc(s_var, 1)

            def norm_b(which, a, w):
                norms[0] += 1
                dve.wait_ge(s_std, norms[0])
                g = a.shape[1]
                link(V.tensor_tensor(a, a, spread(stat[which][1][:, 0:g], w), ALU.mult))

            def flat(a):
                return a.rearrange("p c h e -> p (c h) e")

            def rows(key, pt):
                o = LNO[key][0] + P * pt
                return wide(lnb[:, o:o + P], 2)

            def wide(a, n):
                return a.unsqueeze(1).broadcast_to([P, n] + list(a.shape[1:]))

            dve.wait_ge(s_ptr, 1)
            V.tensor_copy(wsT, pview(5, 0, 4, P))
            V.memset(stat["g"][1], 1.0)
            V.tensor_copy(pcol, bank[4][:, 0:NROWS]).then_inc(s_pev, 1)
            dve.wait_ge(s_pev, 1)
            m0, m1 = pcol[:, ROWS["mu0"]:ROWS["mu0"] + 11], pcol[:, ROWS["mu1"]:ROWS["mu1"] + 11]
            link(V.scalar_tensor_tensor(own, m0, -1.0, m1, ALU.mult, ALU.subtract))
            V.tensor_scalar(own, own, 1.0, None, ALU.add).then_inc(s_pev, 1)

            def shifted(i):
                dve.wait_ge(s_base, i + 1)
                _, _, kind, j = T_TILES[i]
                src, b = bank[i % 4], base[:, i % 2]
                if i < NR:
                    m = MU_COL[kind] + (j if kind in "rkv" else 0)
                    prev, nxt = par("mu0", m), par("mu1", m)
                    dst = {"r": rT, "k": kT, "v": vT}[kind][:, j] if kind in "rkv" else {"wa": wa, "gd": gd}[kind]
                else:
                    prev, nxt = par("cw", j), par("cw", 12 + j)
                    dst = qk[:, j]
                link(V.scalar_tensor_tensor(b[:, 1:S], src[:, 0:S - 1], prev, b[:, 1:S], ALU.mult, ALU.add))
                V.scalar_tensor_tensor(dst[:, 0:S - 1], src[:, 1:S], nxt, b[:, 0:S - 1], ALU.mult, ALU.add)
                V.tensor_copy(dst[:, S - 1:S], b[:, S - 1:S]).then_inc(s_shift, 1)

            for i in range(NR):
                shifted(i)
            dve.wait_ge(s_shift, NR)
            for j in range(NP):
                last = V.tensor_scalar(kkraw[:, j], kT[:, j], par("kk", j), None, ALU.mult)
            link(last)
            V.tensor_tensor(kksq, kkraw, kkraw, ALU.mult).then_inc(s_sq, 1)
            shifted(11)
            shifted(12)
            dve.wait_ge(s_ss, 1)
            kkf = kk.rearrange("p a s -> p (a s)")
            V.tensor_scalar(kkf[:, 0:512], bank[6][:, :], 1e-24, None, ALU.max).then_inc(s_kmx, 1)
            V.tensor_scalar(kkf[:, 512:768], bank[7][:, 0:S], 1e-24, None, ALU.max).then_inc(s_kmx, 1)
            for i in range(13, NT):
                shifted(i)
            dve.wait_ge(s_kkd, 1)
            link(V.reciprocal(kk, kk))
            V.tensor_tensor(kk, kk, kkraw, ALU.mult).then_inc(s_kk2, 1)
            dve.wait_ge(s_kk2, 1)

            def prep_scan(pt):
                dve.wait_ge(s_sig, pt + 1)
                for d in range(2):
                    for c in range(NCH):
                        o = srel[:, d, P * c:P * c + P]
                        i = sigw[:, pt, d, P * c:P * c + P]
                        if d:
                            o, i = o[:, ::-1], i[:, ::-1]
                        last = V.tensor_tensor_scan(o, ones, i, 0.0, ALU.mult, ALU.add)
                link(last)

            def prep_relative(pt):
                s4 = srel.rearrange("p d (c t) -> p d c t", c=NCH)
                V.tensor_scalar(sref[:, 0], s4[:, 0, :, P - 1], 0.5, None, ALU.mult)
                link(V.tensor_scalar(sref[:, 1], s4[:, 1, :, 0], 0.5, None, ALU.mult))
                V.tensor_tensor(gam[:, pt % 2], sref[:, :, 0], sref[:, :, 1], ALU.add)
                sf = srel.rearrange("p d (c t) -> p (d c) t", c=NCH)
                link(V.tensor_tensor(sf, sf, spread(sref.rearrange("p d c -> p (d c)"), P), ALU.subtract))
                V.tensor_tensor(s_exc, srel, sigw[:, pt], ALU.subtract).then_inc(s_rel, 1)

            def prep_keys(pt):
                dve.wait_ge(s_ksc, pt + 1)
                link(V.scalar_tensor_tensor(tmpk, icl[:, pt], -1.0, wide(kka, 2), ALU.add, ALU.mult))
                link(V.tensor_tensor(kdir, tmpk, wide(kT[:, pt], 2), ALU.add))
                link(V.tensor_tensor(kds, kdir[:, 0], kdir[:, 1], ALU.add))
                V.tensor_tensor(bon[:, pt], rrk, kds, ALU.mult).then_inc(s_bon, 1)
                link(V.tensor_tensor(tmpk, icl[:, pt], wide(kk[:, pt], 2), ALU.mult))

            def prep_operands(pt):
                ar = ar_[pt % 2]
                dve.wait_ge(s_exp, pt + 1)
                if pt:
                    dve.wait_ge(s_bk, 2 * pt)

                def by_chunk(a):
                    return a.rearrange("p d (c t) -> p d c t", c=NCH)

                for h in range(2):
                    own_half = hsel[:, h:h + 1]
                    V.scalar_tensor_tensor(ktz[h], by_chunk(kdir), own_half, by_chunk(e_inv), ALU.mult, ALU.mult)
                    V.scalar_tensor_tensor(btz[h], by_chunk(tmpk), own_half, by_chunk(e_inv), ALU.mult, ALU.mult)
                for d in range(2):
                    V.scalar_tensor_tensor(ar[:, d, :, 0], by_chunk(s_exc)[:, d], -1.0,
                                           kk[:, pt].rearrange("p (c t) -> p c t", c=NCH), ALU.mult, ALU.mult)
                    last = V.tensor_tensor(ar[:, d, :, 1], by_chunk(e_inc)[:, d],
                                           rT[:, pt].rearrange("p (c t) -> p c t", c=NCH), ALU.mult)
                last.then_inc(s_ops, 1)

            dve.wait_ge(s_msk_c, 16)
            prep_scan(0)
            prep_relative(0)
            prep_keys(0)
            dve.wait_ge(s_silu, 1)
            V.tensor_tensor(qk[:, 0:3], qk[:, 0:3], sgq[:, 0:3], ALU.mult)
            V.scalar_tensor_tensor(qk[:, 3:6], sgq[:, 3:6], HD ** -0.5, qk[:, 3:6], ALU.mult, ALU.mult).then_inc(s_qk, 1)
            prep_operands(0)
            dve.wait_ge(s_gtr, 1)
            dve.wait_ge(s_small, 64)
            r0, r1, r2, r3 = row0[0:RH], row1[0:RH], row2[0:RH], row3[0:RH]
            for d in range(2):
                V.tensor_scalar(r3[:, d], bank[4][0:RH, S * d:S * d + S], gbias[0:RH, d:d + 1], None, ALU.add)
                last = V.tensor_scalar(r0[:, d], bank[5][0:RH, S * d:S * d + S], gbias[0:RH, 2 + d:3 + d], None, ALU.add)
            link(last)
            V.scalar_tensor_tensor(r1, r0, -1.0, r0, ALU.mult, ALU.max).then_inc(s_grow, 1)

            def gate_rows():
                dve.wait_ge(s_gact, 1)
                link(V.scalar_tensor_tensor(r0, r0, 0.0, r1, ALU.min, ALU.subtract))
                for d in range(2):
                    a, b = r0[:, d], r2[:, d]
                    if d:
                        a, b = a[:, ::-1], b[:, ::-1]
                    on = ones[0:RH, 0:1].broadcast_to([RH, S])
                    last = V.tensor_tensor_scan(b, on, a, 0.0, ALU.mult, ALU.add)
                link(last)
                link(V.tensor_tensor(r3, r3, r2, ALU.subtract))
                for d in range(2):
                    a, b = r3[:, d], r1[:, d]
                    if d:
                        a, b = a[:, ::-1], b[:, ::-1]
                    last = V.tensor_tensor_scan(b, a, a, 0.0, ALU.max, ALU.max)
                link(last)
                V.tensor_tensor(r0, r1, r2, ALU.add).then_inc(s_grow, 1)

            gv = gel[:, :, GW:2 * GW]

            def gmlp_out():
                dve.wait_ge(s_gmix, 1)
                for g in range(4):
                    last = V.scalar_tensor_tensor(grp[:, :, HD * g:HD * g + HD], pview(3, P * g, NCH, HD), par("bs", g),
                                                  gel[:, :, HD * g:HD * g + HD], ALU.add, ALU.mult)
                last.then_inc(s_grp, 1)

            def args(h):
                dve.wait_ge(s_mb, h + 1)
                if h:
                    dve.wait_ge(s_pt, h)
                for d, col, sc, t0, n in ((0, 0, 0, 0, S), (0, S, 1, P, P), (1, 0, 0, 0, P), (1, P, 1, 0, S)):
                    last = V.tensor_scalar(ebuf[:, d, col:col + n], bank[3][:, S * d + t0:S * d + t0 + n],
                                           gcolm[:, d, sc, h:h + 1], 0.0, ALU.subtract, ALU.max)
                last.then_inc(s_arg, 1)

            def weights(h):
                dve.wait_ge(s_sc, h + 1)
                dve.wait_ge(s_dm, h + 1)
                if h:
                    dve.wait_ge(s_pv, h)
                for d, col, src, n in ((0, 0, 0, S), (0, S, S + P, P), (1, 0, 0, P), (1, P, S, S)):
                    last = V.tensor_tensor(pbuf[:, d, col:col + n], ebuf[:, d, col:col + n], bank[3][:, src:src + n], ALU.mult)
                last.then_inc(s_pt, 1)

            def divide(h):
                dve.wait_ge(s_pv, h + 1)
                if h == 0:
                    dve.wait_ge(s_gcev, 1)
                nd = pview(7, 0, 2, NCH, 65)
                link(V.tensor_scalar(den, nd[:, :, :, HD], -1.0, None, ALU.mult))
                link(V.tensor_tensor(den, den, nd[:, :, :, HD], ALU.max))
                link(V.tensor_tensor(den, den, emt[:, :, :, h], ALU.max))
                link(V.reciprocal(rec, den))
                for d in range(2):
                    last = V.tensor_tensor(ntmp[:, d], nd[:, d, :, 0:HD], spread(rec[:, d], HD), ALU.mult)
                link(last)
                V.tensor_tensor(hm[:, :, h % 2], ntmp[:, 0], ntmp[:, 1], ALU.add).then_inc(s_hn, 1)
                dve.wait_ge(s_hn, h + 1)

            def scans_out(pt):
                dve.wait_ge(s_ot, pt + 1)
                V.tensor_copy(orw, pview(7, 0, NCH, 2, HD)).then_inc(s_oev, 1)
                dve.wait_ge(s_oev, pt + 1)

            def mlstm_norm_b(pt):
                norm_b("m", flat(hm), HD)
                h2 = hm.rearrange("p c h e -> p c (h e)")
                link(V.tensor_tensor(h2, h2, rows("mg", pt), ALU.mult))
                V.tensor_tensor(grp[:, :, GW + RW + P * pt:GW + RW + P * pt + P], h2, osig[:, :, P * pt:P * pt + P],
                                ALU.mult).then_inc(s_grp, 1)

            def rwkv_norm_b(pt):
                norm_b("r", flat(orw), HD)
                o2 = orw.rearrange("p c h e -> p c (h e)")
                link(V.tensor_tensor(o2, o2, rows("rg", pt), ALU.mult))
                link(V.tensor_tensor(o2, o2, rows("rb", pt), ALU.add))
                link(V.tensor_tensor(sq, vtok[:, :, P * pt:P * pt + P].rearrange("p c (h e) -> p c h e", h=2),
                                     spread(bsum[:, :, 2 * pt:2 * pt + 2], HD), ALU.mult))
                link(V.tensor_tensor(o2, o2, sq.rearrange("p (c h) e -> p c (h e)", c=NCH), ALU.add))
                V.tensor_tensor(grp[:, :, GW + P * pt:GW + P * pt + P], o2, gate_r[:, :, P * pt:P * pt + P],
                                ALU.mult).then_inc(s_grp, 1)

            dve.wait_ge(s_lnb, 80)
            for pt in range(NP):
                for n, (d, f, b) in enumerate(FILLS):
                    dve.wait_ge(s_prod, 8 * pt + n + 1)
                    h = f % 2
                    V.tensor_tensor((nqT, mpT)[f // 2][:, d, 2 * h:2 * h + 2], pview(4 * d + b, 0, 2, 256),
                                    wide(mask2(d), 2), ALU.mult).then_inc(s_prev, 1)
                for n in range(len(LEVELS)):
                    for d in range(2):
                        dve.wait_ge(s_a, 12 * pt + 2 * n + d + 1)
                        V.tensor_tensor(gm[:, d], pview(4 * d, 0, 4, P), wide(gmask(d, n), 4), ALU.mult).then_inc(s_g, 1)
                    if n == 0:
                        if pt == 0:
                            gate_rows()
                        else:
                            scans_out(pt - 1)
                            norm_a("r", flat(orw), sq, HD, GN_EPS)
                        if pt + 1 < NP:
                            prep_scan(pt + 1)
                    if n == 1:
                        dve.wait_ge(s_bs, pt + 1)
                        if pt == 0:
                            V.tensor_copy(emt, pview(7, 24, 2, NCH, RH)).then_inc(s_gcol, 1)
                            link(V.tensor_copy(gcolm, pview(7, 0, 2, NCH, RH)))
                        V.tensor_copy(bsum[:, :, 2 * pt:2 * pt + 2], pview(7, 64, NCH, 2)).then_inc(s_bev, 1)
                        args(2 * pt)
                        if pt:
                            rwkv_norm_b(pt - 1)
                        if pt + 1 < NP:
                            prep_relative(pt + 1)
                    if n == 2:
                        weights(2 * pt)
                        if pt:
                            norm_a("m", flat(hm), sq, HD, LN_EPS)
                        else:
                            norm_a("g", gv, gsq, GW, LN_EPS)
                        if pt + 1 < NP:
                            prep_keys(pt + 1)
                    if n == 3:
                        if pt:
                            mlstm_norm_b(pt - 1)
                        else:
                            norm_b("g", gv, GW)
                            link(V.tensor_tensor(gv, gv, wide(lnb[:, 0:GW], 2), ALU.mult))
                            V.tensor_tensor(gv, gv, wide(lnb[:, GW:2 * GW], 2), ALU.add).then_inc(s_gv, 1)
                        args(2 * pt + 1)
                        if pt:
                            dve.wait_ge(s_grp, 2 * pt)
                        divide(2 * pt)
                    if n == 4:
                        weights(2 * pt + 1)
                    if n == 5:
                        divide(2 * pt + 1)
                        if pt + 1 < NP:
                            prep_operands(pt + 1)
                        else:
                            gmlp_out()
            norm_a("m", flat(hm), sq, HD, LN_EPS)
            mlstm_norm_b(NP - 1)
            scans_out(NP - 1)
            norm_a("r", flat(orw), sq, HD, GN_EPS)
            rwkv_norm_b(NP - 1)

            def layer_norm(c, which, src):
                a = [x_tok[:, c, 512 * hf:512 * hf + 512] for hf in range(2)]
                for hf in range(2):
                    last = V.bn_stats(bns[:, c, hf], src[hf])
                link(last)
                link(V.bn_aggr(mvar[:, c], bns[:, c].rearrange("p a b -> p (a b)")))
                V.tensor_scalar(mvar[:, c, 1:2], mvar[:, c, 1:2], LN_EPS, None, ALU.add).then_inc(s_var2, 1)
                for hf in range(2):
                    last = V.scalar_tensor_tensor(a[hf], src[hf], mvar[:, c, 0:1],
                                                  ln4[:, 2 * which, 512 * hf:512 * hf + 512], ALU.subtract, ALU.mult)
                link(last)
                dve.wait_ge(s_std2, 2 * which + c + 1)
                return V.scalar_tensor_tensor(x_tok[:, c], x_tok[:, c], mvar[:, c, 1:2], ln4[:, 2 * which + 1],
                                              ALU.mult, ALU.add)

            dve.wait_ge(s_late, 16 * 4)
            for c in range(NCH):
                dve.wait_ge(s_mix, 2 * c + 2)
                for hf in range(2):
                    xh = x_tok[:, c, 512 * hf:512 * hf + 512]
                    last = V.scalar_tensor_tensor(xh, xh, ALPHA, bank[4 + 2 * c + hf][:, :], ALU.mult, ALU.add)
                link(last)
                layer_norm(c, 0, [x_tok[:, c, 0:512], x_tok[:, c, 512:1024]]).then_inc(s_x1, 1)

            iota = cst[:, C_IOTA:C_IOTA + P]
            V.tensor_scalar(al_id, ident, ALPHA, None, ALU.mult).then_inc(s_al, 1)
            for i in range(MAXPASS):
                V.tensor_copy(hot[0:NE, NE * i:NE * i + NE], ident[0:NE, 0:NE])
            link(V.memset(hot[0:NE, NE * MAXPASS:], 0.0))
            V.tensor_scalar(esel[0:NE], ones[0:NE, 0:SLOTS], hot[0:NE, 0:1], None, ALU.mult).then_inc(s_esel, 1)

            dve.wait_ge(s_lg, 1)
            link(V.tensor_tensor(lg, pview(4, 0, NCH, NE), wide(rb, NCH), ALU.add))
            for c in range(NCH):
                last = V.max(mx[:, c], lg[:, c])
            link(last)
            v4 = mx[:, :, TOPK - 1:TOPK].broadcast_to([P, NCH, NE])
            V.tensor_scalar(small[:, 0:2], mx[:, :, 0], -1.0, None, ALU.mult).then_inc(s_rexp_in, 1)
            V.tensor_tensor(mgt, lg, v4, ALU.is_gt)
            link(V.tensor_tensor(meq, lg, v4, ALU.is_equal))
            V.tensor_reduce(small[:, 4:6], mgt, X, ALU.add)
            for c in range(NCH):
                last = V.tensor_tensor_scan(mcum[:, c], ones[:, 0:NE], meq[:, c], 0.0, ALU.mult, ALU.add)
            link(last)
            link(V.tensor_scalar(small[:, 4:6], small[:, 4:6], -1.0, float(TOPK), ALU.mult, ALU.add))
            link(V.tensor_tensor(mcum, mcum, spread(small[:, 4:6], NE), ALU.is_le))
            link(V.tensor_tensor(meq, meq, mcum, ALU.mult))
            V.tensor_tensor(msk, mgt, meq, ALU.add).then_inc(s_msk, 1)
            dve.wait_ge(s_msk, 1)
            dve.wait_ge(s_rexp, 1)
            link(V.tensor_tensor(gates, gates, msk, ALU.mult))
            link(V.tensor_reduce(small[:, 8:10], gates, X, ALU.add))
            link(V.reciprocal(small[:, 8:10], small[:, 8:10]))
            link(V.tensor_tensor(gates, gates, spread(small[:, 8:10], NE), ALU.mult))
            dve.wait_ge(s_pos, 1)
            link(V.scalar_tensor_tensor(mcum, pview(5, 0, NCH, NE), 1.0, msk, ALU.add, ALU.mult))
            for i in range(MAXPASS):
                last = V.tensor_scalar(posm[:, :, NE * i:NE * i + NE], mcum, -1.0 - SLOTS * i, None, ALU.add)
                if i == 0:
                    link(last)
                    for c in range(NCH):
                        last = V.tensor_scalar(sel[:, c], iota[:, 0:SLOTS], posm[:, c, 0:1], None, ALU.is_equal)
                    last.then_inc(s_sel, 1)
            for i in range(MAXPASS):
                V.tensor_copy(gatex[:, :, NE * i:NE * i + NE], gates)
            V.memset(posm[:, :, NE * MAXPASS:], -1.0)
            link(V.memset(gatex[:, :, NE * MAXPASS:], 0.0))
            V.tensor_reduce(small[:, 12:13], bank[5][:, 2 * NE:3 * NE], X, ALU.max).then_inc(s_moe, 1)
            dve.wait_ge(s_moe, 1)
            link(V.tensor_scalar(small[:, 16:17], small[:, 12:13], float(SLOTS), None, ALU.is_gt))
            for i in range(2, MAXPASS):
                link(V.scalar_tensor_tensor(small[:, 16:17], small[:, 12:13], float(SLOTS * i), small[:, 16:17],
                                            ALU.is_gt, ALU.add))
            V.tensor_scalar(npass_i[:, :], small[:, 16:17], 1.0, None, ALU.add).then_inc(s_moe, 1)
            dve.wait_ge(s_moe, 2)
            npass = dve.value_load(npass_i[0:1, 0:1], min_val=1, max_val=MAXPASS)
            with dve.Fori(0, npass) as p:
                with dve.Fori(0, NE) as e:
                    it = p * NE + e
                    dve.wait_ge(s_w1, it * 4 + 1)
                    for c in range(NCH):
                        last = V.tensor_scalar(gsel[:, c], iota, posm[:, c, bass.ds(it, 1)],
                                               gatex[:, c, bass.ds(it, 1)], ALU.is_equal, ALU.mult)
                    last.then_inc(s_gsel, 1)
                    for c in range(NCH):
                        last = V.tensor_scalar(sel[:, c], iota[:, 0:SLOTS], posm[:, c, bass.ds(it + 1, 1)], None,
                                               ALU.is_equal)
                    last.then_inc(s_sel, 1)
                    dve.wait_ge(s_w1, it * 4 + 4)
                    V.tensor_scalar(hr, bank[4][:, :], 7.0, None, ALU.min).then_inc(s_hg, 1)
                    V.tensor_scalar(ur, bank[5][:, :], 7.0, -7.0, ALU.min, ALU.max).then_inc(s_hu, 1)
                    dve.wait_ge(s_hs, it + 1)
                    V.tensor_tensor(hr, hr, sg, ALU.mult).then_inc(s_hm, 1)
                    dve.wait_ge(s_hu, it + 1)
                    dve.wait_ge(s_hm, it + 1)
                    V.scalar_tensor_tensor(hr, ur, 1.0, hr, ALU.add, ALU.mult).then_inc(s_ht, 1)
                    dve.wait_ge(s_esu, it + 1)
                    V.tensor_scalar(esel[0:NE], ones[0:NE, 0:SLOTS], hot[0:NE, bass.ds(it + 1, 1)], None,
                                    ALU.mult).then_inc(s_esel, 1)
            dve.wait_ge(s_late2, 32)
            for c in range(NCH):
                dve.wait_ge(s_all, c + 1)
                layer_norm(c, 1, [bank[2 * c + hf][:, :] for hf in range(2)]).then_inc(s_fin, 1)


_INS = ["x", "w_in", "gmlp_ln_g", "gmlp_ln_b", "gmlp_ws", "gmlp_bs", "rwkv_mu", "rwkv_w0", "rwkv_w2", "rwkv_a0",
        "rwkv_a2", "rwkv_g2", "rwkv_k_k", "rwkv_k_a", "rwkv_r_k", "rwkv_ln_g", "rwkv_ln_b", "mlstm_conv_w",
        "mlstm_conv_b", "mlstm_gate_b", "mlstm_ln_g", "w_out", "ln1_g", "ln1_b", "router_w", "router_b",
        "exp_w1", "exp_b1", "exp_w2", "exp_b2", "ln2_g", "ln2_b"]
DEBUG = False


def kernel(**inputs):
    import concourse.bacc as bacc
    from concourse.bass_utils import run_bass_kernel_spmd

    nc = bacc.Bacc("TRN2", target_bir_lowering=False, num_devices=1)
    f32 = mybir.dt.float32
    arrays, t = {}, {}
    for name in _INS:
        a = np.ascontiguousarray(inputs[name])
        arrays[f"in_{name}"] = a
        t[name] = nc.dram_tensor(f"in_{name}", a.shape, mybir.dt.from_np(a.dtype), kind="ExternalInput").ap()
    arrays["in_consts"] = constants()
    t["consts"] = nc.dram_tensor("in_consts", (P, NCONST), f32, kind="ExternalInput").ap()
    out = nc.dram_tensor("out", (1, S, D), f32, kind="ExternalOutput").ap()
    dbg = {"grp": nc.dram_tensor("dbg_grp", (S, D), f32, kind="ExternalOutput").ap()} if DEBUG else None
    encoder_kernel(nc, t, out, dbg)
    r = run_bass_kernel_spmd(nc, [arrays], core_ids=[0])
    return r.results[0]["out"]
```
